# Optimizing a Trainium2 kernel written in Bass

```python
import math
import jax, jax.numpy as jnp
from jax import lax
import numpy as np

D_MODEL = 1024
BATCH = 1
SEQ = 256
DEPTH = 1

MEM_LEN = 256
HEAD_DIM = 64
MIX_WIDTH = D_MODEL
DA_WIDTH = MIX_WIDTH // 2
SB_WIDTH = MIX_WIDTH - DA_WIDTH
DA_HEADS = DA_WIDTH // (2 * HEAD_DIM)
DA_V = 2 * HEAD_DIM
SB_HEADS = SB_WIDTH // HEAD_DIM
DA_Q_COLS = DA_HEADS * 2 * HEAD_DIM
DA_K_COLS = DA_HEADS * 2 * HEAD_DIM
DA_V_COLS = DA_HEADS * DA_V
SB_COLS = SB_HEADS * HEAD_DIM
IN_COLS = DA_Q_COLS + DA_K_COLS + DA_V_COLS + 3 * SB_COLS
ROT_DIM = HEAD_DIM // 4
ROPE_THETA = 500000.0
X_HEADS = 4
X_HEAD_DIM = D_MODEL // X_HEADS
D_FF = 4 * D_MODEL
Q_BLOCK = 128
EPS = 1e-6


def rms_norm(x, g):
    xf = x.astype(jnp.float32)
    y = xf * lax.rsqrt(jnp.mean(xf * xf, axis=-1, keepdims=True) + EPS)
    return (y * g.astype(jnp.float32)).astype(x.dtype)

def rope_tables(positions, dtype):
    inv_freq = ROPE_THETA ** (-jnp.arange(0, ROT_DIM, 2, dtype=jnp.float32) / ROT_DIM)
    ang = positions.astype(jnp.float32)[..., None] * inv_freq
    return jnp.cos(ang).astype(dtype), jnp.sin(ang).astype(dtype)

def apply_partial_rope(x, cos, sin):
    extra = x.ndim - 3
    c = cos.reshape(cos.shape[:2] + (1,) * extra + cos.shape[-1:])
    s = sin.reshape(sin.shape[:2] + (1,) * extra + sin.shape[-1:])
    half = ROT_DIM // 2
    x1, x2, xp = x[..., :half], x[..., half:ROT_DIM], x[..., ROT_DIM:]
    return jnp.concatenate([x1 * c - x2 * s, x2 * c + x1 * s, xp], axis=-1)

def diff_attention(q, k, v, lam, g_subln, lam_init):
    B, S, H = q.shape[0], q.shape[1], q.shape[2]
    nb = S // Q_BLOCK
    scale = 1.0 / math.sqrt(HEAD_DIM)
    kh = k.transpose(0, 2, 3, 1, 4)
    vh = v.transpose(0, 2, 1, 3).astype(jnp.float32)
    qb = q.transpose(0, 2, 3, 1, 4).reshape(B, H, 2, nb, Q_BLOCK, HEAD_DIM)
    qb = jnp.moveaxis(qb, 3, 0)
    qidx = jnp.arange(S, dtype=jnp.int32).reshape(nb, Q_BLOCK)
    kidx = jnp.arange(S, dtype=jnp.int32)

    def block(args):
        qblk, qi = args
        s = jnp.einsum('bhcqd,bhckd->bhcqk', qblk, kh).astype(jnp.float32) * scale
        mask = kidx[None, :] <= qi[:, None]
        p = jax.nn.softmax(jnp.where(mask, s, -jnp.inf), axis=-1)
        w = p[:, :, 0] - lam * p[:, :, 1]
        return jnp.einsum('bhqk,bhkv->bhqv', w, vh)

    o = lax.map(block, (qb, qidx))
    o = o.transpose(1, 0, 3, 2, 4).reshape(B, S, H, DA_V)
    o = rms_norm(o, g_subln) * (1.0 - lam_init)
    return o.reshape(B, S, H * DA_V)

def stick_breaking_attention(q, k, v):
    B, S, H = q.shape[0], q.shape[1], q.shape[2]
    nb = S // Q_BLOCK
    scale = 1.0 / math.sqrt(HEAD_DIM)
    kh = k.transpose(0, 2, 1, 3)
    vh = v.transpose(0, 2, 1, 3).astype(jnp.float32)
    qb = q.transpose(0, 2, 1, 3).reshape(B, H, nb, Q_BLOCK, HEAD_DIM)
    qb = jnp.moveaxis(qb, 2, 0)
    qidx = jnp.arange(S, dtype=jnp.int32).reshape(nb, Q_BLOCK)
    kidx = jnp.arange(S, dtype=jnp.int32)

    def block(args):
        qblk, qi = args
        z = jnp.einsum('bhqd,bhkd->bhqk', qblk, kh).astype(jnp.float32) * scale
        strict = kidx[None, :] < qi[:, None]
        log_beta = jax.nn.log_sigmoid(z)
        log_1mb = jnp.where(strict, jax.nn.log_sigmoid(-z), 0.0)
        between = lax.cumsum(log_1mb, axis=3, reverse=True) - log_1mb
        a = jnp.exp(jnp.where(strict, log_beta + between, -jnp.inf))
        return jnp.einsum('bhqk,bhkd->bhqd', a, vh)

    o = lax.map(block, (qb, qidx))
    return o.transpose(1, 0, 3, 2, 4).reshape(B, S, H * HEAD_DIM)

def cross_attention(h, memn, w_xq, w_xkv, w_xo):
    B, S, _ = h.shape
    q = (h @ w_xq).reshape(B, S, X_HEADS, X_HEAD_DIM)
    kv = memn @ w_xkv
    k = kv[..., :D_MODEL].reshape(B, MEM_LEN, X_HEADS, X_HEAD_DIM)
    v = kv[..., D_MODEL:].reshape(B, MEM_LEN, X_HEADS, X_HEAD_DIM).astype(jnp.float32)
    s = jnp.einsum('bqhd,bkhd->bhqk', q, k).astype(jnp.float32) / math.sqrt(X_HEAD_DIM)
    p = jax.nn.softmax(s, axis=-1)
    o = jnp.einsum('bhqk,bkhd->bqhd', p, v).reshape(B, S, D_MODEL).astype(h.dtype)
    return o @ w_xo

def first_inputs(seed: int = 0) -> dict:
    key = jax.random.key(seed)
    ks = jax.random.split(key, 24)
    f32 = jnp.float32

    def w(k, shape, fan_in):
        return jax.random.normal(k, shape, f32) * (fan_in ** -0.5)

    def gain(k, shape):
        return 1.0 + 0.02 * jax.random.normal(k, shape, f32)

    L = DEPTH
    return {
        "x": jax.random.normal(ks[0], (BATCH, SEQ, D_MODEL), f32),
        "mem": jax.random.normal(ks[1], (BATCH, MEM_LEN, D_MODEL), f32),
        "positions": jnp.broadcast_to(jnp.arange(SEQ, dtype=jnp.int32), (BATCH, SEQ)),
        "g_mix": gain(ks[2], (L, D_MODEL)),
        "w_in": w(ks[3], (L, D_MODEL, IN_COLS), D_MODEL),
        "lambda_q1": 0.1 * jax.random.normal(ks[4], (L, HEAD_DIM), f32),
        "lambda_k1": 0.1 * jax.random.normal(ks[5], (L, HEAD_DIM), f32),
        "lambda_q2": 0.1 * jax.random.normal(ks[6], (L, HEAD_DIM), f32),
        "lambda_k2": 0.1 * jax.random.normal(ks[7], (L, HEAD_DIM), f32),
        "g_subln": gain(ks[8], (L, DA_V)),
        "w_out": w(ks[9], (L, MIX_WIDTH, D_MODEL), MIX_WIDTH),
        "g_cross": gain(ks[10], (L, D_MODEL)),
        "g_mem": gain(ks[11], (L, D_MODEL)),
        "w_xq": w(ks[12], (L, D_MODEL, D_MODEL), D_MODEL),
        "w_xkv": w(ks[13], (L, D_MODEL, 2 * D_MODEL), D_MODEL),
        "w_xo": w(ks[14], (L, D_MODEL, D_MODEL), D_MODEL),
        "g_mlp": gain(ks[15], (L, D_MODEL)),
        "w_up": w(ks[16], (L, D_MODEL, D_FF), D_MODEL),
        "w_down": w(ks[17], (L, D_FF, D_MODEL), D_FF),
        "g_final": gain(ks[18], (D_MODEL,)),
    }

def first_block(x, mem, positions, g_mix, w_in, lambda_q1, lambda_k1, lambda_q2, lambda_k2,
              g_subln, w_out, g_cross, g_mem, w_xq, w_xkv, w_xo, g_mlp, w_up, w_down,
              g_final):
    B, S, _ = x.shape
    cos, sin = rope_tables(positions, x.dtype)
    h = x
    for l in range(DEPTH):
        lam_init = 0.8 - 0.6 * math.exp(-0.3 * l)
        u = rms_norm(h, g_mix[l]) @ w_in[l]
        o0 = 0
        qa = u[..., o0:o0 + DA_Q_COLS].reshape(B, S, DA_HEADS, 2, HEAD_DIM); o0 += DA_Q_COLS
        ka = u[..., o0:o0 + DA_K_COLS].reshape(B, S, DA_HEADS, 2, HEAD_DIM); o0 += DA_K_COLS
        va = u[..., o0:o0 + DA_V_COLS].reshape(B, S, DA_HEADS, DA_V); o0 += DA_V_COLS
        qs = u[..., o0:o0 + SB_COLS].reshape(B, S, SB_HEADS, HEAD_DIM); o0 += SB_COLS
        ksb = u[..., o0:o0 + SB_COLS].reshape(B, S, SB_HEADS, HEAD_DIM); o0 += SB_COLS
        vs = u[..., o0:o0 + SB_COLS].reshape(B, S, SB_HEADS, HEAD_DIM)
        qa = apply_partial_rope(qa, cos, sin)
        ka = apply_partial_rope(ka, cos, sin)
        lam = (jnp.exp(jnp.sum(lambda_q1[l].astype(jnp.float32) * lambda_k1[l].astype(jnp.float32)))
               - jnp.exp(jnp.sum(lambda_q2[l].astype(jnp.float32) * lambda_k2[l].astype(jnp.float32)))
               + lam_init)
        ya = diff_attention(qa, ka, va, lam, g_subln[l], lam_init)
        yb = stick_breaking_attention(qs, ksb, vs)
        y = jnp.concatenate([ya.astype(h.dtype), yb.astype(h.dtype)], axis=-1)
        h = h + y @ w_out[l]
        h = h + cross_attention(rms_norm(h, g_cross[l]), rms_norm(mem, g_mem[l]),
                                w_xq[l], w_xkv[l], w_xo[l])
        a = jnp.square(jax.nn.relu(rms_norm(h, g_mlp[l]) @ w_up[l]))
        h = h + a @ w_down[l]
    return rms_norm(h, g_final)


ROPE_THETA_2 = 10000.0
NORM_EPS = 1e-6
NEG = -1e30
NSA_HEADS = 12
NSA_KV_GROUPS = 3
NSA_HPG = NSA_HEADS // NSA_KV_GROUPS
CMP_BLOCK = 32
CMP_STRIDE = 16
CMP_HIDDEN = 256
SLC_BLOCK = 64
SLC_TOPK = 16
WIN_SIZE = 512
SLC_Q_BLOCK = 64
WIN_Q_BLOCK = 128
DIL_PAIRS = ((128, 1), (512, 4), (2048, 16))
DIL_GROUPS = len(DIL_PAIRS)
DIL_HPG = 4
DIL_HEADS = DIL_GROUPS * DIL_HPG
DIL_NKEYS = max(w // d + 1 for w, d in DIL_PAIRS)
DIL_Q_BLOCK = 128
D_FF_2 = 4 * D_MODEL
Q_A_COLS = NSA_HEADS * HEAD_DIM
KV_A_COLS = NSA_KV_GROUPS * HEAD_DIM
GATE_A_COLS = 3 * NSA_HEADS
QKV_B_COLS = DIL_HEADS * HEAD_DIM
IN_SIZES = (Q_A_COLS, KV_A_COLS, KV_A_COLS, KV_A_COLS, KV_A_COLS, KV_A_COLS, KV_A_COLS,
            GATE_A_COLS, QKV_B_COLS, QKV_B_COLS, QKV_B_COLS, D_MODEL, D_MODEL)
IN_COLS_2 = sum(IN_SIZES)
SPLIT_POINTS = tuple(int(c) for c in np.cumsum(IN_SIZES)[:-1])


def _rmsnorm(x, g):
    xf = x.astype(jnp.float32)
    y = xf * lax.rsqrt(jnp.mean(xf * xf, axis=-1, keepdims=True) + NORM_EPS)
    return (y * g.astype(jnp.float32)).astype(x.dtype)

def _rope(x, pos):
    half = HEAD_DIM // 2
    inv_freq = jnp.power(ROPE_THETA_2, -jnp.arange(half, dtype=jnp.float32) / half)
    ang = jnp.asarray(pos, jnp.float32)[:, None] * inv_freq[None, :]
    shape = (1, ang.shape[0]) + (1,) * (x.ndim - 3) + (half,)
    cos = jnp.cos(ang).reshape(shape)
    sin = jnp.sin(ang).reshape(shape)
    xf = x.astype(jnp.float32)
    x1, x2 = xf[..., :half], xf[..., half:]
    return jnp.concatenate([x1 * cos - x2 * sin, x2 * cos + x1 * sin], axis=-1).astype(x.dtype)

def _masked_softmax(s, mask):
    s = jnp.where(mask, s.astype(jnp.float32), NEG)
    return jax.nn.softmax(s, axis=-1) * mask

def _compress(kv, pos_emb, w1, w2):
    B, S, G, dh = kv.shape
    n_cmp = (S - CMP_BLOCK) // CMP_STRIDE + 1
    idx = np.arange(n_cmp)[:, None] * CMP_STRIDE + np.arange(CMP_BLOCK)[None, :]
    blocks = kv[:, idx] + pos_emb[None, None, :, None, :]
    blocks = jnp.transpose(blocks, (0, 1, 3, 2, 4)).reshape(B, n_cmp, G, CMP_BLOCK * dh)
    return jax.nn.gelu(blocks @ w1) @ w2

def _cmp_to_slc_overlap(n_cmp, n_slc):
    cs = np.arange(n_cmp)[:, None] * CMP_STRIDE
    ss = np.arange(n_slc)[None, :] * SLC_BLOCK
    ov = np.minimum(cs + CMP_BLOCK, ss + SLC_BLOCK) - np.maximum(cs, ss)
    return (np.clip(ov, 0, None) / CMP_BLOCK).astype(np.float32)

def _nsa_mixer(q, k_cmp, v_cmp, k_slc, v_slc, k_win, v_win, gate,
               k_norm_cmp, cmp_k_pos, cmp_k_w1, cmp_k_w2, cmp_v_pos, cmp_v_w1, cmp_v_w2):
    B, S = q.shape[0], q.shape[1]
    G, R, dh = NSA_KV_GROUPS, NSA_HPG, HEAD_DIM
    scale = dh ** -0.5
    t = np.arange(S)

    kc = _compress(k_cmp, cmp_k_pos, cmp_k_w1, cmp_k_w2)
    vc = _compress(v_cmp, cmp_v_pos, cmp_v_w1, cmp_v_w2)
    n_cmp = kc.shape[1]
    c_end = np.arange(n_cmp) * CMP_STRIDE + CMP_BLOCK - 1
    kc = _rope(_rmsnorm(kc, k_norm_cmp), c_end)
    s_cmp = jnp.einsum("bsgrd,bcgd->bgrsc", q, kc) * scale
    p_cmp = _masked_softmax(s_cmp, c_end[None, :] <= t[:, None])
    o_cmp = jnp.einsum("bgrsc,bcgd->bsgrd", p_cmp.astype(vc.dtype), vc)

    n_slc = S // SLC_BLOCK
    top_n = min(SLC_TOPK, n_slc)
    overlap = jnp.asarray(_cmp_to_slc_overlap(n_cmp, n_slc))
    imp = jnp.einsum("bgrsc,cn->bgsn", p_cmp, overlap)
    blk = np.arange(n_slc)[None, :]
    cur = (t // SLC_BLOCK)[:, None]
    forced = (blk == 0) | (blk == cur) | (blk == cur - 1)
    score = jnp.where(forced, jnp.inf, jnp.where(blk <= cur, imp, -jnp.inf))
    top_score, top_idx = lax.top_k(score, top_n)
    top_ok = top_score > -jnp.inf

    kb = jnp.transpose(k_slc.reshape(B, n_slc, SLC_BLOCK, G, dh), (0, 3, 1, 2, 4))
    vb = jnp.transpose(v_slc.reshape(B, n_slc, SLC_BLOCK, G, dh), (0, 3, 1, 2, 4))
    gather_blocks = jax.vmap(jax.vmap(lambda kk, ii: kk[ii]))
    nqs = S // SLC_Q_BLOCK

    def slc_block(xs):
        qc, idx, ok, tq = xs
        ks = gather_blocks(kb, idx)
        vs = gather_blocks(vb, idx)
        s = jnp.einsum("bqgrd,bgqnkd->bgrqnk", qc, ks) * scale
        kpos = idx[..., None] * SLC_BLOCK + np.arange(SLC_BLOCK)
        mask = ok[..., None] & (kpos <= tq[:, None, None])
        s = s.reshape(B, G, R, SLC_Q_BLOCK, top_n * SLC_BLOCK)
        mask = mask.reshape(B, G, 1, SLC_Q_BLOCK, top_n * SLC_BLOCK)
        p = _masked_softmax(s, mask)
        vs = vs.reshape(B, G, SLC_Q_BLOCK, top_n * SLC_BLOCK, dh)
        return jnp.einsum("bgrqj,bgqjd->bqgrd", p.astype(vs.dtype), vs)

    qs = jnp.moveaxis(q.reshape(B, nqs, SLC_Q_BLOCK, G, R, dh), 1, 0)
    idx_s = jnp.moveaxis(top_idx.reshape(B, G, nqs, SLC_Q_BLOCK, top_n), 2, 0)
    ok_s = jnp.moveaxis(top_ok.reshape(B, G, nqs, SLC_Q_BLOCK, top_n), 2, 0)
    tq_s = jnp.arange(S, dtype=jnp.int32).reshape(nqs, SLC_Q_BLOCK)
    o_slc = lax.map(slc_block, (qs, idx_s, ok_s, tq_s))
    o_slc = jnp.moveaxis(o_slc, 0, 1).reshape(B, S, G, R, dh)

    span = WIN_SIZE + WIN_Q_BLOCK
    kw_pad = jnp.pad(k_win, ((0, 0), (WIN_SIZE, 0), (0, 0), (0, 0)))
    vw_pad = jnp.pad(v_win, ((0, 0), (WIN_SIZE, 0), (0, 0), (0, 0)))
    nqw = S // WIN_Q_BLOCK

    def win_block(xs):
        qc, start = xs
        ks = lax.dynamic_slice_in_dim(kw_pad, start, span, axis=1)
        vs = lax.dynamic_slice_in_dim(vw_pad, start, span, axis=1)
        s = jnp.einsum("bqgrd,bkgd->bgrqk", qc, ks) * scale
        tq = start + jnp.arange(WIN_Q_BLOCK)
        kp = start - WIN_SIZE + jnp.arange(span)
        diff = tq[:, None] - kp[None, :]
        mask = (diff >= 0) & (diff < WIN_SIZE) & (kp[None, :] >= 0)
        p = _masked_softmax(s, mask)
        return jnp.einsum("bgrqk,bkgd->bqgrd", p.astype(vs.dtype), vs)

    qw = jnp.moveaxis(q.reshape(B, nqw, WIN_Q_BLOCK, G, R, dh), 1, 0)
    starts = jnp.arange(nqw, dtype=jnp.int32) * WIN_Q_BLOCK
    o_win = lax.map(win_block, (qw, starts))
    o_win = jnp.moveaxis(o_win, 0, 1).reshape(B, S, G, R, dh)

    y = gate[..., 0:1] * o_cmp + gate[..., 1:2] * o_slc + gate[..., 2:3] * o_win
    return y.reshape(B, S, G * R * dh)

def _dilated_mixer(q, k, v):
    B, S = q.shape[0], q.shape[1]
    dh = HEAD_DIM
    scale = dh ** -0.5
    dil = np.array([d for _, d in DIL_PAIRS])
    win = np.array([w for w, _ in DIL_PAIRS])
    j = np.arange(DIL_NKEYS)
    in_window = (j[None, :] * dil[:, None]) <= win[:, None]
    kg = jnp.transpose(k, (2, 0, 1, 3, 4))
    vg = jnp.transpose(v, (2, 0, 1, 3, 4))
    gather_stride = jax.vmap(lambda kk, ii: kk[:, ii])
    nq = S // DIL_Q_BLOCK

    def dil_block(xs):
        qc, tq = xs
        kpos = tq[None, :, None] - j[None, None, :] * dil[:, None, None]
        mask = (kpos >= 0) & in_window[:, None, :]
        idx = jnp.maximum(kpos, 0)
        ks = gather_stride(kg, idx)
        vs = gather_stride(vg, idx)
        s = jnp.einsum("gbqhd,gbqjhd->gbhqj", qc, ks).astype(jnp.float32) * scale
        s = jnp.where(mask[:, None, None], s, NEG)
        m = jnp.max(s, axis=-1, keepdims=True)
        e = jnp.exp(s - m)
        den = jnp.sum(e, axis=-1, keepdims=True)
        o = jnp.einsum("gbhqj,gbqjhd->gbqhd", (e / den).astype(vs.dtype), vs)
        lse = (m + jnp.log(den))[..., 0]
        w = jax.nn.softmax(lse, axis=0)
        return jnp.einsum("gbhq,gbqhd->bqhd", w.astype(o.dtype), o)

    qd = jnp.moveaxis(jnp.transpose(q, (2, 0, 1, 3, 4)).reshape(DIL_GROUPS, B, nq, DIL_Q_BLOCK, DIL_HPG, dh), 2, 0)
    tq_d = jnp.arange(S, dtype=jnp.int32).reshape(nq, DIL_Q_BLOCK)
    o = lax.map(dil_block, (qd, tq_d))
    return jnp.moveaxis(o, 0, 1).reshape(B, S, DIL_HPG * dh)

def second_inputs(seed: int = 0) -> dict:
    key = jax.random.key(seed)
    ks = jax.random.split(key, 21)
    L = DEPTH

    def nrm(k, shape, scale):
        return scale * jax.random.normal(k, shape, jnp.float32)

    def gain(k, n):
        return 1.0 + 0.02 * jax.random.normal(k, (L, n), jnp.float32)

    return {
        "x": jax.random.normal(ks[0], (BATCH, SEQ, D_MODEL), jnp.float32),
        "norm1_g": gain(ks[1], D_MODEL),
        "w_in": nrm(ks[2], (L, D_MODEL, IN_COLS_2), D_MODEL ** -0.5),
        "q_norm_a": gain(ks[3], HEAD_DIM),
        "k_norm_cmp": gain(ks[4], HEAD_DIM),
        "k_norm_slc": gain(ks[5], HEAD_DIM),
        "k_norm_win": gain(ks[6], HEAD_DIM),
        "cmp_k_pos": nrm(ks[7], (L, CMP_BLOCK, HEAD_DIM), 0.2),
        "cmp_k_w1": nrm(ks[8], (L, CMP_BLOCK * HEAD_DIM, CMP_HIDDEN), (CMP_BLOCK * HEAD_DIM) ** -0.5),
        "cmp_k_w2": nrm(ks[9], (L, CMP_HIDDEN, HEAD_DIM), CMP_HIDDEN ** -0.5),
        "cmp_v_pos": nrm(ks[10], (L, CMP_BLOCK, HEAD_DIM), 0.2),
        "cmp_v_w1": nrm(ks[11], (L, CMP_BLOCK * HEAD_DIM, CMP_HIDDEN), (CMP_BLOCK * HEAD_DIM) ** -0.5),
        "cmp_v_w2": nrm(ks[12], (L, CMP_HIDDEN, HEAD_DIM), CMP_HIDDEN ** -0.5),
        "q_norm_b": gain(ks[13], HEAD_DIM),
        "k_norm_b": gain(ks[14], HEAD_DIM),
        "w_o_a": nrm(ks[15], (L, Q_A_COLS, D_MODEL), Q_A_COLS ** -0.5),
        "w_o_b": nrm(ks[16], (L, DIL_HPG * HEAD_DIM, D_MODEL), (DIL_HPG * HEAD_DIM) ** -0.5),
        "w_out": nrm(ks[17], (L, D_MODEL, D_MODEL), D_MODEL ** -0.5),
        "norm2_g": gain(ks[18], D_MODEL),
        "w_up": nrm(ks[19], (L, D_MODEL, D_FF_2), D_MODEL ** -0.5),
        "w_down": nrm(ks[20], (L, D_FF_2, D_MODEL), D_FF_2 ** -0.5),
    }

def second_block(x, norm1_g, w_in, q_norm_a, k_norm_cmp, k_norm_slc, k_norm_win,
              cmp_k_pos, cmp_k_w1, cmp_k_w2, cmp_v_pos, cmp_v_w1, cmp_v_w2,
              q_norm_b, k_norm_b, w_o_a, w_o_b, w_out, norm2_g, w_up, w_down):
    B, S = x.shape[0], x.shape[1]
    G, R, dh = NSA_KV_GROUPS, NSA_HPG, HEAD_DIM
    pos = np.arange(S)
    for i in range(DEPTH):
        h = _rmsnorm(x, norm1_g[i])
        proj = h @ w_in[i]
        (q_a, k_c, v_c, k_s, v_s, k_w, v_w, g_nsa,
         q_b, k_b, v_b, g_ma, g_mb) = jnp.split(proj, SPLIT_POINTS, axis=-1)

        q_a = _rope(_rmsnorm(q_a.reshape(B, S, NSA_HEADS, dh), q_norm_a[i]), pos).reshape(B, S, G, R, dh)
        k_c = k_c.reshape(B, S, G, dh)
        v_c = v_c.reshape(B, S, G, dh)
        k_s = _rope(_rmsnorm(k_s.reshape(B, S, G, dh), k_norm_slc[i]), pos)
        v_s = v_s.reshape(B, S, G, dh)
        k_w = _rope(_rmsnorm(k_w.reshape(B, S, G, dh), k_norm_win[i]), pos)
        v_w = v_w.reshape(B, S, G, dh)
        g_nsa = jax.nn.sigmoid(g_nsa).reshape(B, S, G, R, 3)
        y_a = _nsa_mixer(q_a, k_c, v_c, k_s, v_s, k_w, v_w, g_nsa,
                         k_norm_cmp[i], cmp_k_pos[i], cmp_k_w1[i], cmp_k_w2[i],
                         cmp_v_pos[i], cmp_v_w1[i], cmp_v_w2[i])

        q_b = _rope(_rmsnorm(q_b.reshape(B, S, DIL_HEADS, dh), q_norm_b[i]), pos)
        k_b = _rope(_rmsnorm(k_b.reshape(B, S, DIL_HEADS, dh), k_norm_b[i]), pos)
        y_b = _dilated_mixer(q_b.reshape(B, S, DIL_GROUPS, DIL_HPG, dh),
                             k_b.reshape(B, S, DIL_GROUPS, DIL_HPG, dh),
                             v_b.reshape(B, S, DIL_GROUPS, DIL_HPG, dh))

        mixed = jax.nn.sigmoid(g_ma) * (y_a @ w_o_a[i]) + jax.nn.sigmoid(g_mb) * (y_b @ w_o_b[i])
        x = x + mixed @ w_out[i]

        h2 = _rmsnorm(x, norm2_g[i])
        x = x + jnp.square(jax.nn.relu(h2 @ w_up[i])) @ w_down[i]
    return x


def setup_inputs(seed=0):
    out = dict(first_inputs(seed))
    for name, value in second_inputs(seed + 1).items():
        if name != "x":
            out[name + "_2"] = value
    return out


def reference(
    x, mem, positions, g_mix, w_in, lambda_q1, lambda_k1, lambda_q2, lambda_k2, g_subln, w_out,
    g_cross, g_mem, w_xq, w_xkv, w_xo, g_mlp, w_up, w_down, g_final, norm1_g_2, w_in_2,
    q_norm_a_2, k_norm_cmp_2, k_norm_slc_2, k_norm_win_2, cmp_k_pos_2, cmp_k_w1_2, cmp_k_w2_2,
    cmp_v_pos_2, cmp_v_w1_2, cmp_v_w2_2, q_norm_b_2, k_norm_b_2, w_o_a_2, w_o_b_2, w_out_2,
    norm2_g_2, w_up_2, w_down_2,
):
    x = first_block(
        x, mem, positions, g_mix, w_in, lambda_q1, lambda_k1, lambda_q2, lambda_k2, g_subln,
        w_out, g_cross, g_mem, w_xq, w_xkv, w_xo, g_mlp, w_up, w_down, g_final,
    )
    return second_block(
        x, norm1_g_2, w_in_2, q_norm_a_2, k_norm_cmp_2, k_norm_slc_2, k_norm_win_2, cmp_k_pos_2,
        cmp_k_w1_2, cmp_k_w2_2, cmp_v_pos_2, cmp_v_w1_2, cmp_v_w2_2, q_norm_b_2, k_norm_b_2,
        w_o_a_2, w_o_b_2, w_out_2, norm2_g_2, w_up_2, w_down_2,
    )


_drawn_inputs = setup_inputs


def setup_inputs(seed=0):
    import zlib

    import numpy as np

    out = dict(_drawn_inputs(seed))
    spreads = {}
    factors = {'lambda_k1': 3.127,
     'lambda_q2': 3.306,
     'g_subln': 4.834,
     'g_cross': 8.0,
     'g_mem': 8.0,
     'g_mlp': 3.211,
     'norm1_g_2': 7.557,
     'q_norm_a_2': 8.0,
     'k_norm_cmp_2': 8.0,
     'k_norm_slc_2': 8.0,
     'k_norm_win_2': 8.0,
     'cmp_k_pos_2': 5.913,
     'q_norm_b_2': 8.0,
     'k_norm_b_2': 8.0,
     'norm2_g_2': 8.825,
     'cmp_v_pos_2': 6.064}
    for name, (base, spread) in spreads.items():
        noise = np.random.default_rng([zlib.crc32(name.encode()), seed]).standard_normal(out[name].shape)
        drawn = base * np.exp(spread * noise) if base else spread * noise
        out[name] = __import__('jax').numpy.asarray(drawn.astype(out[name].dtype))
    for name, factor in factors.items():
        out[name] = (out[name] * factor).astype(out[name].dtype)
    return out
```

```python
import math
from contextlib import ExitStack

import numpy as np

import concourse.bass as bass
from concourse import mybir

D = 1024
S = 256
P = 128
NT = S // P
KT = D // P
HD = 64
EPS = 1e-6
NEG = -1e30
FF = 4 * D
CMP_N = (S - 32) // 16 + 1
NH_A, NG_A = 12, 3
DIL = ((128, 1), (512, 4), (2048, 16))
QA, KC, VC, KS, VS, KW, VW, GA, QB, KB, VB, GM = (
    0, 768, 960, 1152, 1344, 1536, 1728, 1920, 1956, 2724, 3492, 4260)
LAM_INIT = 0.8 - 0.6 * math.exp(-0.3 * 0)
BIG = 12582912.0

C_ID, C_TRI, C_ONE = 0, 128, 256
C_CS2, C_SN2 = 384, 448
C_CMA, C_CMM = 512, 542
C_KCC, C_KCS = 572, 604
C_INV = 636
C_SMALL = 644
C_CAUS, C_STR, C_DIL = 644, 772, 900
C_ALL = C_DIL + 3 * 384


def constants():
    f = np.float32
    c = np.zeros((P, C_ALL), f)
    i = np.arange(P)
    c[:, C_ID:C_ID + P] = np.eye(P)
    c[:, C_TRI:C_TRI + P] = np.where(i[:, None] >= i[None, :], -1.0, 0.0)
    c[:, C_ONE:C_ONE + P] = -1.0
    inv = np.power(f(10000.0), -np.arange(32, dtype=f) / f(32)).astype(f)
    for t in range(NT):
        ang = (np.arange(t * P, t * P + P, dtype=f)[:, None] * inv[None, :]).astype(f)
        c[:, C_CS2 + 32 * t:C_CS2 + 32 * t + 32] = np.cos(ang)
        c[:, C_SN2 + 32 * t:C_SN2 + 32 * t + 32] = np.sin(ang)
        ok = (16 * np.arange(CMP_N) + 31)[None, :] <= (t * P + i)[:, None]
        c[:, C_CMA + 15 * t:C_CMA + 15 * t + 15] = np.where(ok, 0.0, NEG)
        c[:, C_CMM + 15 * t:C_CMM + 15 * t + 15] = ok
    ang = ((16 * np.arange(CMP_N) + 31).astype(f)[:, None] * inv[None, :]).astype(f)
    c[:CMP_N, C_KCC:C_KCC + 32] = np.cos(ang)
    c[:CMP_N, C_KCS:C_KCS + 32] = np.sin(ang)
    c[:, C_INV:C_INV + 8] = np.power(f(500000.0), -np.arange(0, 16, 2, dtype=f) / f(16))
    c[:, C_CAUS:C_CAUS + P] = np.where(i[None, :] <= i[:, None], 0.0, NEG)
    c[:, C_STR:C_STR + P] = np.where(i[None, :] > i[:, None], 0.0, NEG)
    for g, (win, dil) in enumerate(DIL):
        for t in range(NT):
            d = (t * P + i)[:, None] - np.arange((t + 1) * P)[None, :]
            ok = (d >= 0) & (d % dil == 0) & (d <= win)
            at = C_DIL + 384 * g + P * t
            c[:, at:at + P * (t + 1)] = np.where(ok, 0.0, NEG)
    return c


def build(nc, a, out):
    f32, f32r, bf16, i32 = (mybir.dt.float32, mybir.dt.float32r, mybir.dt.bfloat16, mybir.dt.int32)
    ALU, ACT, AX = mybir.AluOpType, mybir.ActivationFunctionType, mybir.AxisListType
    ctx = ExitStack()
    with ctx:
        def sb(name, shape, dt=f32):
            return ctx.enter_context(nc.sbuf_tensor(name, shape, dt))

        names = []

        def sem(name):
            names.append(name)
            return ctx.enter_context(nc.semaphore(name))

        RAW = [sb(f"raw{i}", [P, 2048]) for i in range(3)]
        HI = [sb(f"w_hi{i}", [P, 4096], f32r) for i in range(2)]
        LO = [sb(f"w_lo{i}", [P, 4096], f32r) for i in range(2)]
        XH = [sb(f"x_hi{i}", [P, 2048], f32r) for i in range(2)]
        XL = [sb(f"x_lo{i}", [P, 2048], f32r) for i in range(2)]
        xn = sb("xn", [P, NT, D])
        h = sb("h", [P, NT, D])
        gbuf = [sb(f"gain{i}", [P, D]) for i in range(2)]
        cst = sb("cst", [P, C_SMALL])
        mbf = sb("mbf", [P, P + C_ALL - C_SMALL], bf16)
        AR = sb("arena", [P, 16712])
        ST = sb("small", [P, 1710])
        posi = sb("posi", [P, NT], i32)
        PS = ctx.enter_context(nc.psum_tensor("ps", [P, 4096], f32))

        st_at = [0]

        def small(n):
            st_at[0] += n
            assert st_at[0] <= 1710, st_at[0]
            return ST[:, st_at[0] - n:st_at[0]]

        def bank(b, n=1):
            return PS[:, 512 * b:512 * (b + n)]

        ident = cst[:, C_ID:C_ID + P]
        tri = cst[:, C_TRI:C_TRI + P]
        negones = cst[:, C_ONE:C_ONE + P]
        identb = mbf[:, 0:P]

        def maskb(col, n):
            return mbf[:, P + col - C_SMALL:P + col - C_SMALL + n]

        u_qa, u_ka, u_va, u_vs = (AR[:, 1024 * i:1024 * i + 1024].rearrange("p (t c) -> p t c", t=NT)
                                  for i in range(4))
        qaT, kaT, qsT, ksT = (AR[:, 4096 + 1024 * i:5120 + 1024 * i] for i in range(4))
        kmT = AR[:, 8192:10240]
        vm = AR[:, 10240:12288].rearrange("p (t c) -> p t c", t=NT)
        memx = vm
        pr1 = [AR[:, 12288 + 512 * i:12800 + 512 * i] for i in range(4)]
        sbz = [AR[:, 0:768], AR[:, 14336:15104]]
        sba = [AR[:, 768:1536], AR[:, 15104:15872]]
        comb1 = AR[:, 15872:16384]
        sq1 = AR[:, 12288:13312]
        qxT = AR[:, 0:2048]
        u2 = AR[:, 0:2 * GM].rearrange("p (t c) -> p t c", t=NT)
        qT = AR[:, 8520:10056]
        kT = AR[:, 10056:11592]
        qbT = AR[:, 11592:13128]
        kbT = AR[:, 13128:14664]
        kdup = [AR[:, 11592:12360], AR[:, 12360:13128]]
        cdup = AR[:, 13128:14664]
        kc2 = AR[:, 11592:13128]
        AT = AR[:, 13128:14568]
        pc = AR[:, 11592:12360]
        pcT = AR[:, 12360:13128]
        pr2 = [AR[:, 14664 + 512 * i:15176 + 512 * i] for i in range(4)]
        ta = AR[:, 14664:16200]
        act_q = AR[:, 14664:15688]
        comb2 = gbuf[1][:, 0:256]
        sqb = xn[:, :, :].rearrange("p t c -> p (t c)")[:, 0:1536]

        eps = small(1)
        marks = small(40)
        ss_n, y0_n, nr_n = small(14), small(14), small(14)
        t_nr1, t_nr2 = small(48), small(48)
        rstd_n = small(14)
        den, nmx = small(160), small(160)
        coef = small(4)
        lamv = AR[:, 14848:15104]
        lamp = AR[:, 15104:15232]
        lams = small(2)
        lame = small(2)
        nlam = small(1)
        gsub = small(128)
        ss_s, y0_s, rs_s = small(8), small(8), small(8)
        posf = small(2)
        ang = small(32)
        rn = small(32)
        scs = small(32)
        rp = AR[:, 14336:14848]
        gq = small(6 * 64)
        T1, T2 = gbuf[1][:, 256:384], gbuf[1][:, 384:512]
        ss_h, y0_h, rs_h = small(24), small(24), small(24)
        pe2 = small(32)
        vecs = small(128)
        w2sb = sb("w2sb", [P, 2, 2, 64])
        sgn = small(72)
        smax = small(24)
        cden = small(24)
        dl = [small(24) for _ in range(4)]
        d8 = [small(8) for _ in range(3)]
        cwork = AR[:, 14664:16200]
        hx, hu, hg = cwork[:, 0:180], cwork[:, 180:360], cwork[:, 360:540]
        kcn = cwork[0:15, 0:192]
        kcd = cwork[0:15, 192:576]
        vcr = cwork[:, 576:768]
        kcT = cwork[:, 768:816]
        ktmp = cwork[:, 816:1008]
        scb = cwork[:, 1008:1368]

        raw_loaded = [sem(f"raw_loaded{i}") for i in range(3)]
        x_loaded, mem_loaded, cst_loaded = sem("x_loaded"), sem("mem_loaded"), sem("cst_loaded")
        msk_loaded, misc_loaded = sem("msk_loaded"), sem("misc_loaded")
        gain_loaded = [sem(f"gain_loaded{i}") for i in range(7)]
        out_stored = sem("out_stored")
        hi_done = sem("hi_done")
        lo_done = sem("lo_done")
        raw_used = sem("raw_used")
        strip_done = sem("strip_done")
        evac_done = sem("evac_done")
        tb_done = sem("tb_done")
        tb_hi = sem("tb_hi")
        tb_evac = sem("tb_evac")
        xn_ready = sem("xn_ready")
        norm_sq = sem("norm_sq")
        norm_used = sem("norm_used")
        src_ready = sem("src_ready")
        masks_ready = sem("masks_ready")
        rope_arg = sem("rope_arg")
        rope_sin = sem("rope_sin")
        lam_arg, lam_exp = sem("lam_arg"), sem("lam_exp")
        qk_ready = sem("qk_ready")
        sc_done = sem("sc_done")
        mx_done = sem("mx_done")
        ex_done = sem("ex_done")
        tr_done = sem("tr_done")
        pt_done = sem("pt_done")
        pv_done = sem("pv_done")
        post_done = sem("post_done")
        sub_sq, sub_y0 = sem("sub_sq"), sem("sub_y0")
        z_done, z_ln = sem("z_done"), sem("z_ln")
        z_sp, z_cum, z_at, z_pv = sem("z_sp"), sem("z_cum"), sem("z_at"), sem("z_pv")
        up_evac = sem("up_evac")
        sq_ready = sem("sq_ready")
        a_hi, a_lo = sem("a_hi"), sem("a_lo")
        hn_sq, hn_ss, hn_y0, hn_done = sem("hn_sq"), sem("hn_ss"), sem("hn_y0"), sem("hn_done")
        at_ready, ge_arg, ge_exp, hid_ready = (sem("at_ready"), sem("ge_arg"), sem("ge_exp"),
                                               sem("hid_ready"))
        kc_ss, kc_y0, kc_ready = sem("kc_ss"), sem("kc_y0"), sem("kc_ready")
        sg_arg, sg_exp = sem("sg_arg"), sem("sg_exp")
        cs_arg, cs_exp, pc_ready = sem("cs_arg"), sem("cs_exp"), sem("pc_ready")
        dl_den, dl_ln, dl_arg, dl_exp = sem("dl_den"), sem("dl_ln"), sem("dl_arg"), sem("dl_exp")
        gates_in, gates_sig = sem("gates_in"), sem("gates_sig")
        row_step = sem("row_step")
        dve_step = sem("dve_step")
        act_step = sem("act_step")
        res_done = sem("res_done")

        strips, halves = [], []

        def col_strip(w, c0, width, mode, x):
            src = w[0].rearrange("(k p) n -> p k n", p=P)
            strips.append(dict(mode=mode, w=width, x=x))
            for q in range(2):
                halves.append(("split", src[:, 4 * q:4 * q + 4, c0:c0 + width], 4 * width, len(strips) - 1))

        def row_strip(parts, x, k0, first=False, last=False, mode="acc"):
            strips.append(dict(mode=mode, w=D, x=x, k0=k0, first=first, last=last))
            for w, r0 in parts:
                src = w[0, r0:r0 + 2 * P, :].rearrange("(k p) n -> p k n", p=P)
                halves.append(("split", src, 2048, len(strips) - 1))

        def mlp_strips(up, down, x, ax):
            def u(j):
                col_strip(up, 512 * j, 512, "up", x)
                strips[-1]["j"] = j

            def d(j):
                row_strip([(down, 512 * j), (down, 512 * j + 256)], ax, 4 * (j % 2), j == 0, j == 7, "down")
                strips[-1]["j"] = j
            u(0)
            for j in range(1, 8):
                u(j)
                d(j - 1)
            d(7)

        for c, mode in enumerate(("tok", "tok", "tok", "T", "T", "tok")):
            col_strip(a["w_in"], 512 * c, 512, mode, 0)
        for c in range(4):
            col_strip(a["w_xkv"], 512 * c, 512, "T" if c < 2 else "tok", 1)
        for c in range(2):
            row_strip([(a["w_out"], 512 * c), (a["w_out"], 512 * c + 256)], 0, 4 * c, c == 0, c == 1)
        for c in range(2):
            col_strip(a["w_xq"], 512 * c, 512, "T", 1)
        for c in range(2):
            row_strip([(a["w_xo"], 512 * c), (a["w_xo"], 512 * c + 256)], 0, 4 * c, c == 0, c == 1)
        MLP1 = len(strips)
        mlp_strips(a["w_up"], a["w_down"], 1, 0)
        IN2 = len(strips)
        for c in range(9):
            if c == 7:
                for kv in ("cmp_k_w1_2", "cmp_v_w1_2"):
                    src = a[kv][0].rearrange("(k p) n -> p k n", p=P)
                    for q in range(2):
                        halves.append(("raw", src[:, 8 * q:8 * q + 8, :], 2048, None))
            col_strip(a["w_in_2"], 512 * c, min(512, GM - 512 * c), "tok", 1)
        for c in range(4):
            col_strip(a["w_in_2"], GM + 512 * c, 512, "tok", 1)
        row_strip([(a["w_o_a_2"], 0), (a["w_o_a_2"], 256)], 0, 0, True, False)
        row_strip([(a["w_o_a_2"], 512), (a["w_o_b_2"], 0)], 0, 4, False, True, "mixed")
        for c in range(2):
            row_strip([(a["w_out_2"], 512 * c), (a["w_out_2"], 512 * c + 256)], 1, 4 * c, c == 0, c == 1)
        MLP2 = len(strips)
        mlp_strips(a["w_up_2"], a["w_down_2"], 0, 1)
        NS = len(strips)
        raw_of, half_of, n_split = [], {}, 0
        for n, (kind, _, _, s) in enumerate(halves):
            if kind == "split":
                half_of.setdefault(s, []).append(n)
                n_split += 1
        split_before = [sum(k == "split" for k, *_ in halves[:n]) for n in range(len(halves) + 1)]
        raw_before = [n - split_before[n] for n in range(len(halves) + 1)]
        raw_halves = [n for n, hf in enumerate(halves) if hf[0] == "raw"]

        evacs, pair_user, turn = 0, {0: 0, 1: 0, 2: 0, 3: 0}, 0
        for s, d in enumerate(strips):
            if d["mode"] in ("tok", "T"):
                d["pair"] = 2 * (turn % 2) if not 6 <= s <= 9 else 0
                turn += 1
                banks = [d["pair"], d["pair"] + 1]
            elif d["mode"] == "up":
                continue
            else:
                banks = [0, 1, 2, 3]
            d["need_evac"] = max(pair_user[b] for b in banks)
            if d["mode"] in ("tok", "T") or d["last"]:
                evacs += 1
                d["evac"] = evacs
                for b in banks:
                    pair_user[b] = evacs

        def up_strip(base, j):
            return base + (0 if j == 0 else 2 * j - 1)

        def down_strip(base, j):
            return base + (15 if j == 7 else 2 * j + 2)

        units = []

        def seg_base(n):
            return 4 * n

        for t, hs in [(0, (0, 1)), (0, (2, 3)), (1, (0,)), (1, (1,)), (1, (2,)), (1, (3,))]:
            w = P * (t + 1)
            segs = []
            for hh in hs:
                for c in range(2):
                    r = slice(64 * c, 64 * c + 64)
                    segs.append(dict(
                        row=64 * c, qk=[(qaT[r, 256 * hh + P * t:256 * hh + P * t + P], kaT[r, 256 * hh:256 * hh + w])],
                        mask=[(w - P, maskb(C_CAUS, P))],
                        v=[u_va[:, k, P * hh:P * hh + P] for k in range(t + 1)], vw=P))
            units.append(dict(kind="diff", t=t, hs=hs, w=w, segs=segs, pr=pr1))
        U_X = len(units)
        for t in range(NT):
            for pair in range(2):
                segs = []
                for hh in (2 * pair, 2 * pair + 1):
                    segs.append(dict(
                        row=0, qk=[(qxT[:, 256 * k + P * t:256 * k + P * t + P], kmT[:, 256 * k:256 * k + 256])
                            for k in (2 * hh, 2 * hh + 1)],
                        mask=[], v=[vm[:, k, 256 * hh:256 * hh + 256] for k in range(NT)], vw=256))
                units.append(dict(kind="cross", t=t, hs=(2 * pair, 2 * pair + 1), w=256, segs=segs, pr=pr1))
        U_A = len(units)
        for t in range(NT):
            w = P * (t + 1)
            for u in range(6 if t == 0 else 12):
                hs = (2 * u, 2 * u + 1) if t == 0 else (u,)
                segs = []
                for hh in hs:
                    r = slice(64 * (hh % 2), 64 * (hh % 2) + 64)
                    g = hh // 4
                    for b, vcol in ((0, VS), (1, VW)):
                        kc = 768 * b + 256 * g
                        segs.append(dict(
                            row=r.start, qk=[(qT[r, 256 * (hh // 2) + P * t:256 * (hh // 2) + P * t + P], kT[r, kc:kc + w])],
                            mask=[(w - P, maskb(C_CAUS, P))],
                            v=[u2[:, k, vcol + 64 * g:vcol + 64 * g + 64] for k in range(t + 1)], vw=64))
                units.append(dict(kind="nsa", t=t, hs=hs, w=w, segs=segs, pr=pr2))
        U_D = len(units)
        for t in range(NT):
            w = P * (t + 1)
            n = 4 if t == 0 else 2
            for u in range(12 // n):
                hs = tuple(range(n * u, n * u + n))
                segs = []
                for hh in hs:
                    r = slice(64 * (hh % 2), 64 * (hh % 2) + 64)
                    g = hh // 4
                    segs.append(dict(
                        row=r.start, qk=[(qbT[r, 256 * (hh // 2) + P * t:256 * (hh // 2) + P * t + P],
                             kbT[r, 256 * (hh // 2):256 * (hh // 2) + w])],
                        mask=[(0, maskb(C_DIL + 384 * g + P * t, w))],
                        v=[u2[:, k, VB + 64 * hh:VB + 64 * hh + 64] for k in range(t + 1)], vw=64))
                units.append(dict(kind="dil", t=t, hs=hs, w=w, segs=segs, pr=pr2))
        NU = len(units)
        dil_den, dil_nm = small(24), small(24)

        def den_of(n):
            u = units[n]
            if u["kind"] == "dil":
                b = 12 * u["t"] + u["hs"][0]
                return dil_den[:, b:b + len(u["segs"])], dil_nm[:, b:b + len(u["segs"])]
            return den[:, 4 * n:4 * n + len(u["segs"])], nmx[:, 4 * n:4 * n + len(u["segs"])]

        NORMS = ["g_mix", "g_mem", "g_cross", "g_mlp", "g_final", "norm1_g_2", "norm2_g_2"]

        FILLS = [(0, 0), (1, 0), (0, 6), (1, 10), (0, 12), (1, 14), (1, MLP1 + 14),
                 (0, MLP1 + 16), (1, IN2 + 13), (0, IN2 + 15)]

        def gain_src(g):
            v = a[NORMS[g]]
            v = v if len(v.shape) == 1 else v[0]
            return v.partition_broadcast(P)

        def raw_wait(eng, n):
            eng.wait_ge(raw_loaded[n % 3], 16 * (n // 3 + 1))

        block = ctx.enter_context(nc.Block())

        @block.sync
        def _(sp):
            sp.dma_start(h[:, :, :], a["x"].rearrange("o (t p) d -> p (o t) d", p=P)).then_inc(x_loaded, 16)
            gains_at = {18: 2, 26: 3, 38: 4, 44: 5, half_of[IN2 + 13][0]: 6}
            for n, (kind, src, size, s) in enumerate(halves):
                if n in gains_at:
                    g = gains_at[n]
                    sp.wait_ge(norm_used, g - 1)
                    sp.dma_start(gbuf[g % 2][:, :], gain_src(g)).then_inc(gain_loaded[g], 16)
                if n >= 3:
                    if halves[n - 3][0] == "split":
                        sp.wait_ge(lo_done, split_before[n - 2])
                    else:
                        sp.wait_ge(raw_used, (raw_before[n - 2] + 1) // 2)
                dst = RAW[n % 3][:, 0:size].rearrange("p (k n) -> p k n", k=src.shape[1])
                sp.dma_start(dst, src).then_inc(raw_loaded[n % 3], 16)
            sp.wait_ge(res_done, 1)
            sp.dma_start(out.rearrange("o (t p) d -> p (o t) d", p=P), h[:, :, :]).then_inc(out_stored, 16)
            sp.wait_ge(out_stored, 16)

        @block.gpsimd
        def _(pool):
            for s in range(NS):
                for q, n in enumerate(half_of[s]):
                    size = halves[n][2]
                    pool.wait_ge(hi_done, split_before[n] + 1)
                    c = slice(2048 * q, 2048 * q + size)
                    nc.gpsimd.tensor_tensor(LO[s % 2][:, c], RAW[n % 3][:, 0:size],
                                            HI[s % 2][:, c].bitcast(f32), ALU.subtract).then_inc(lo_done, 1)

        @block.scalar
        def _(act):
            chain = [0]

            def link(ins):
                chain[0] += 1
                ins.then_inc(act_step, 1)
                act.wait_ge(act_step, chain[0])

            act.dma_start(gbuf[0][:, :], gain_src(0)).then_inc(gain_loaded[0], 16)
            act.dma_start(cst[:, :], a["cst"][:, 0:C_SMALL]).then_inc(cst_loaded, 16)
            act.dma_start(memx, a["mem"].rearrange("o (t p) d -> p (o t) d", p=P)).then_inc(mem_loaded, 16)
            act.dma_start(gbuf[1][:, :], gain_src(1)).then_inc(gain_loaded[1], 16)
            act.dma_start(AR[:, 0:C_ALL - C_SMALL], a["cst"][:, C_SMALL:C_ALL]).then_inc(msk_loaded, 16)
            misc = []
            for n, name in enumerate(("lambda_q1", "lambda_q2", "lambda_k1", "lambda_k2")):
                misc.append((lamv[:, 64 * n:64 * n + 64], a[name][0].partition_broadcast(P)))
            misc.append((gsub, a["g_subln"][0].partition_broadcast(P)))
            for n, name in enumerate(("q_norm_a_2", "k_norm_slc_2", "k_norm_win_2", "q_norm_b_2",
                                      "k_norm_b_2", "k_norm_cmp_2")):
                misc.append((gq[:, 64 * n:64 * n + 64], a[name][0].partition_broadcast(P)))
            for n, name in enumerate(("cmp_k_pos_2", "cmp_v_pos_2")):
                misc.append((vecs[16 * n:16 * n + 16, :], a[name][0].rearrange("(t q) d -> t (q d)", q=2)))
            for n, name in enumerate(("cmp_k_w2_2", "cmp_v_w2_2")):
                misc.append((w2sb[:, n, :, :], a[name][0].rearrange("(k p) n -> p k n", p=P)))
            with nc.allow_non_contiguous_dma(reason="one position per partition"):
                misc.append((posi[:, :], a["positions"][0].rearrange("(t p) -> p t", p=P)))
                for dst, src in misc:
                    act.dma_start(dst, src).then_inc(misc_loaded, 16)

            def norm_stats(i, src):
                act.wait_ge(norm_used, i)
                for t in range(NT):
                    nc.scalar.activation(xn[:, t, :], src[:, t, :], ACT.Square,
                                         accum_out=ss_n[:, 2 * i + t:2 * i + t + 1]).then_inc(act_step, 1)
                    chain[0] += 1
                act.wait_ge(act_step, chain[0])
                c = slice(2 * i, 2 * i + 2)
                link(nc.scalar.activation(nr_n[:, c], ss_n[:, c], ACT.Ln, scale=1.0 / D, bias=eps))
                nc.scalar.activation(y0_n[:, c], nr_n[:, c], ACT.Exp, scale=-0.5).then_inc(norm_sq, 1)

            strip_n = [0]

            def hi(s):
                assert s == strip_n[0]
                strip_n[0] += 1
                if s >= 2:
                    act.wait_ge(strip_done, s - 1)
                for q, n in enumerate(half_of[s]):
                    size = halves[n][2]
                    raw_wait(act, n)
                    nc.scalar.activation(HI[s % 2][:, 2048 * q:2048 * q + size], RAW[n % 3][:, 0:size],
                                         ACT.Copy).then_inc(hi_done, 1)

            tb = [0]
            fill = [0]

            def fill_hi():
                buf, done = FILLS[fill[0]]
                act.wait_ge(strip_done, done)
                for b in range(4):
                    t, kh = b // 2, b % 2
                    act.wait_ge(tb_done, tb[0] + 1)
                    dst = XH[buf][:, 1024 * kh:1024 * kh + 1024].rearrange("p (k u) -> p k u", u=S)
                    src = bank(4 + tb[0] % 4).rearrange("p (k u) -> p k u", u=P)
                    nc.scalar.activation(dst[:, :, P * t:P * t + P], src, ACT.Copy).then_inc(tb_hi, 1)
                    tb[0] += 1
                fill[0] += 1

            def exps(n):
                u = units[n]
                dn, nm = den_of(n)
                act.wait_ge(mx_done, n + 1)
                if n >= 2:
                    act.wait_ge(tr_done, n - 1)
                last = len(u["segs"]) - 1
                for i in range(last + 1):
                    c = slice(u["w"] * i, u["w"] * i + u["w"])
                    x = nc.scalar.activation(u["pr"][n % 2][:, c], bank(4 + n % 2)[:, c], ACT.Exp,
                                             bias=nm[:, i:i + 1], accum_out=dn[:, i:i + 1])
                    if i == last:
                        x.then_inc(ex_done, 1)

            act.wait_ge(x_loaded, 16)
            act.wait_ge(rope_arg, 1)
            norm_stats(0, h)
            hi(0)
            fill_hi()
            hi(1)
            act.wait_ge(rope_arg, 2)
            nc.scalar.activation(scs, ang, ACT.Sin).then_inc(rope_sin, 1)
            act.wait_ge(lam_arg, 1)
            nc.scalar.activation(lame, lams, ACT.Exp).then_inc(lam_exp, 1)
            act.wait_ge(mem_loaded, 16)
            act.wait_ge(tb_done, 4)
            norm_stats(1, memx)
            hi(2)
            tb[0] = 4
            fill_hi()
            hi(3)
            hi(4)
            tb[0] += 4
            hi(5)
            hi(6)
            hi(7)
            for n in range(U_X):
                exps(n)
                if n == 3:
                    hi(8)
            act.wait_ge(sub_sq, 1)
            link(nc.scalar.activation(y0_s, ss_s, ACT.Ln, scale=1.0 / P, bias=eps))
            nc.scalar.activation(y0_s, y0_s, ACT.Exp, scale=-0.5).then_inc(sub_y0, 1)
            hi(9)
            for half in range(2):
                for j in (2 * half, 2 * half + 1):
                    act.wait_ge(z_done, j + 1)
                    if j >= 2:
                        act.wait_ge(z_cum, j - 1)
                    z = sbz[j % 2]
                    link(nc.scalar.activation(z, bank(4 + 2 * (j % 2), 2)[:, 0:768], ACT.Abs))
                    link(nc.scalar.activation(z, z, ACT.Exp, scale=-1.0))
                    nc.scalar.activation(z, z, ACT.Ln, bias=1.0).then_inc(z_ln, 1)
                for j in (2 * half, 2 * half + 1):
                    act.wait_ge(z_cum, j + 1)
                    if j >= 2:
                        act.wait_ge(z_pv, j - 1)
                    nc.scalar.activation(sba[j % 2], bank(4 + 2 * (j % 2), 2)[:, 0:768], ACT.Exp).then_inc(z_at, 1)
                hi(10 + half)
            fill_hi()
            hi(12)
            act.wait_ge(src_ready, 1)
            norm_stats(2, h)
            hi(13)
            fill_hi()
            hi(14)
            hi(15)
            for n in range(U_X, U_A):
                exps(n)
            fill_hi()
            hi(16)
            act.wait_ge(src_ready, 2)
            norm_stats(3, h)
            hi(17)
            fill_hi()

            def mlp(base, a0, abuf, before):
                for i in range(2, 16):
                    hi(base + i)
                    for j in range(8):
                        if up_strip(0, j) == i - 2:
                            act.wait_ge(sq_ready, a0 + j + 1)
                            act.wait_ge(strip_done, down_strip(base, j - 2) + 1 if j >= 2 else before)
                            c = slice(1024 * (j % 2), 1024 * (j % 2) + 1024)
                            nc.scalar.activation(XH[abuf][:, c], act_q, ACT.Copy).then_inc(a_hi, 1)

            mlp(MLP1, 0, 0, MLP1)
            hi(IN2)
            act.wait_ge(src_ready, 3)
            norm_stats(4, h)
            act.wait_ge(src_ready, 4)
            norm_stats(5, h)
            hi(IN2 + 1)
            fill_hi()

            def head_stats(i, col, heads):
                v = sqb[:, 0:128 * heads].rearrange("p (t c) -> p t c", t=NT)
                if i:
                    act.wait_ge(hn_done, i)
                nc.scalar.activation(v, u2[:, :, col:col + 64 * heads], ACT.Square).then_inc(hn_sq, 1)
                act.wait_ge(hn_ss, i + 1)
                m = 2 * heads
                link(nc.scalar.activation(y0_h[:, 0:m], ss_h[:, 0:m], ACT.Ln, scale=1.0 / HD, bias=eps))
                nc.scalar.activation(y0_h[:, 0:m], y0_h[:, 0:m], ACT.Exp, scale=-0.5).then_inc(hn_y0, 1)

            hi(IN2 + 2)
            hi(IN2 + 3)
            act.wait_ge(evac_done, strips[IN2 + 1]["evac"])
            head_stats(0, QA, 12)
            hi(IN2 + 4)
            hi(IN2 + 5)
            act.wait_ge(evac_done, strips[IN2 + 3]["evac"])
            head_stats(1, KS, 3)
            head_stats(2, KW, 3)
            hi(IN2 + 6)
            act.wait_ge(evac_done, strips[IN2 + 5]["evac"])
            head_stats(3, QB, 12)
            hi(IN2 + 7)
            hi(IN2 + 8)
            act.wait_ge(evac_done, strips[IN2 + 6]["evac"])
            head_stats(4, KB, 12)
            act.wait_ge(ge_arg, 1)
            nc.scalar.activation(hu, hu, ACT.Exp).then_inc(ge_exp, 1)
            hi(IN2 + 9)
            hi(IN2 + 10)
            act.wait_ge(sg_arg, 1)
            nc.scalar.activation(sgn, sgn, ACT.Exp, scale=-1.0).then_inc(sg_exp, 1)
            act.wait_ge(kc_ss, 1)
            link(nc.scalar.activation(y0_h[0:15, 0:3], ss_h[0:15, 0:3], ACT.Ln, scale=1.0 / HD, bias=eps[0:15, :]))
            nc.scalar.activation(y0_h[0:15, 0:3], y0_h[0:15, 0:3], ACT.Exp, scale=-0.5).then_inc(kc_y0, 1)
            act.wait_ge(cs_arg, 1)
            nc.scalar.activation(scb[:, :], scb[:, :], ACT.Exp).then_inc(cs_exp, 1)
            for n in range(U_A, NU):
                exps(n)
                for g in range(4):
                    if n == U_A + GATE_STEP[g] + 1 and g < 2:
                        hi(IN2 + 11 + g)
            hi(IN2 + 13)
            act.wait_ge(dl_den, 1)
            nc.scalar.activation(dl[0], dil_den, ACT.Ln).then_inc(dl_ln, 1)
            act.wait_ge(dl_arg, 1)
            nc.scalar.activation(dl[1], dl[1], ACT.Exp).then_inc(dl_exp, 1)
            act.wait_ge(gates_in, 4)
            for c, w in ((QB, 1536), (QA, 512)):
                nc.scalar.activation(u2[:, :, c:c + w], u2[:, :, c:c + w], ACT.Sigmoid).then_inc(gates_sig, 1)
            tb[0] = TB_Y2
            fill_hi()
            hi(IN2 + 14)
            hi(IN2 + 15)
            fill_hi()
            hi(IN2 + 16)
            hi(MLP2)
            act.wait_ge(src_ready, 5)
            norm_stats(6, h)
            hi(MLP2 + 1)
            fill_hi()
            mlp(MLP2, 8, 1, MLP2)

        @block.vector
        def _(dve):
            chain = [0]
            V = nc.vector
            marked = [0]

            def link(ins):
                chain[0] += 1
                ins.then_inc(dve_step, 1)
                dve.wait_ge(dve_step, chain[0])

            def signal(sm, n):
                cell = marks[:, marked[0]:marked[0] + 1]
                marked[0] += 1
                V.tensor_copy(cell, eps).then_inc(sm, n)

            def newton(r, ss, y0, width):
                n = ss.shape[1]
                p = ss.shape[0]
                m, q = t_nr1[0:p, 0:n], t_nr2[0:p, 0:n]
                link(V.tensor_scalar(m, ss, 1.0 / width, EPS, ALU.mult, ALU.add))
                link(V.tensor_tensor(q, y0, y0, ALU.mult))
                link(V.tensor_tensor(q, q, m, ALU.mult))
                link(V.tensor_scalar(q, q, -0.5, 1.5, ALU.mult, ALU.add))
                link(V.tensor_tensor(r, y0, q, ALU.mult))

            def bc(ap, shape):
                return ap.broadcast_to(shape)

            tb = [0]
            fill = [0]

            def norm_apply(i, src, dst, into_xn):
                dve.wait_ge(norm_sq, i + 1)
                dve.wait_ge(gain_loaded[i], 16)
                newton(rstd_n[:, 2 * i:2 * i + 2], ss_n[:, 2 * i:2 * i + 2], y0_n[:, 2 * i:2 * i + 2], D)
                for t in range(NT):
                    x = V.scalar_tensor_tensor(dst[:, t, :], src[:, t, :], rstd_n[:, 2 * i + t:2 * i + t + 1],
                                               gbuf[i % 2][:, :], ALU.mult, ALU.mult)
                    if into_xn:
                        x.then_inc(xn_ready, 1)
                    else:
                        link(x)
                signal(norm_used, 1)

            def fill_lo():
                buf, done = FILLS[fill[0]]
                dve.wait_ge(strip_done, done)
                for b in range(4):
                    t, kh = b // 2, b % 2
                    dve.wait_ge(tb_hi, 4 * fill[0] + b + 1)
                    c = slice(1024 * kh, 1024 * kh + 1024)
                    dst = XL[buf][:, c].rearrange("p (k u) -> p k u", u=S)[:, :, P * t:P * t + P]
                    sub = XH[buf][:, c].bitcast(f32).rearrange("p (k u) -> p k u", u=S)[:, :, P * t:P * t + P]
                    src = bank(4 + tb[0] % 4).rearrange("p (k u) -> p k u", u=P)
                    V.tensor_tensor(dst, src, sub, ALU.subtract).then_inc(tb_evac, 1)
                    tb[0] += 1
                fill[0] += 1

            def tb_take(fn, last=None):
                dve.wait_ge(tb_done, tb[0] + 1)
                fn(bank(4 + tb[0] % 4)).then_inc(tb_evac, 1)
                tb[0] += 1
                dve.wait_ge(tb_evac, tb[0])

            def evac(s, dst, scale=None):
                d = strips[s]
                dve.wait_ge(strip_done, s + 1)
                src = bank(d["pair"], 2)
                if d["mode"] == "tok":
                    src = src.rearrange("p (t c) -> p t c", t=NT)[:, :, 0:d["w"]]
                if scale is None:
                    V.tensor_copy(dst, src).then_inc(evac_done, 1)
                else:
                    V.tensor_scalar(dst, src, scale, None, ALU.mult).then_inc(evac_done, 1)
                dve.wait_ge(evac_done, d["evac"])

            def residual(s, sem_out):
                dve.wait_ge(strip_done, s + 1)
                hf = h[:, :, :].rearrange("p t c -> p (t c)")
                V.tensor_tensor(hf, hf, bank(0, 4), ALU.add).then_inc(evac_done, 1)
                dve.wait_ge(evac_done, strips[s]["evac"])
                signal(sem_out, 1)

            V.memset(eps, EPS).then_inc(rope_arg, 1)
            dve.wait_ge(rope_arg, 1)
            norm_apply(0, h, xn, True)
            fill_lo()
            dve.wait_ge(cst_loaded, 16)
            dve.wait_ge(misc_loaded, 16 * 16)
            link(V.tensor_copy(posf, posi[:, :]))
            inv = cst[:, C_INV:C_INV + 8]
            a2 = ang.rearrange("p (s t f) -> p s t f", s=2, t=NT)
            base = rp[:, 0:32].rearrange("p (s t f) -> p s t f", s=2, t=NT)
            for sc in range(2):
                link(V.tensor_tensor(base[:, sc], bc(posf.unsqueeze(2), [P, NT, 8]),
                                     bc(inv.unsqueeze(1), [P, NT, 8]), ALU.mult))
                link(V.tensor_scalar(rn[:, 16 * sc:16 * sc + 16], rp[:, 16 * sc:16 * sc + 16],
                                     1.0 / (2 * math.pi), 0.25 * sc, ALU.mult, ALU.add))
            link(V.tensor_scalar(rn, rn, BIG, -BIG, ALU.add, ALU.add))
            rem, first = 2 * math.pi, True
            cur = rp[:, 0:32]
            for piece in TWO_PI:
                link(V.scalar_tensor_tensor(ang, rn, -piece, cur, ALU.mult, ALU.add))
                cur = ang
            link(V.tensor_scalar(ang[:, 16:32], ang[:, 16:32], math.pi / 2, None, ALU.add))
            V.tensor_scalar(ang, ang, PI_LOW, -PI_LOW, ALU.min, ALU.max).then_inc(rope_arg, 1)
            link(V.tensor_tensor(lamp, lamv[:, 0:128], lamv[:, 128:256], ALU.mult))
            V.tensor_reduce(lams, lamp.rearrange("p (a c) -> p a c", a=2), AX.X, ALU.add).then_inc(lam_arg, 1)
            dve.wait_ge(msk_loaded, 16)
            V.tensor_copy(mbf[:, P:], AR[:, 0:C_ALL - C_SMALL]).then_inc(masks_ready, 1)
            V.tensor_copy(identb, ident).then_inc(masks_ready, 1)
            dve.wait_ge(masks_ready, 2)
            link(V.tensor_scalar(gsub, gsub, 1.0 - LAM_INIT, None, ALU.mult))
            dve.wait_ge(lam_exp, 1)
            link(V.tensor_tensor(nlam, lame[:, 1:2], lame[:, 0:1], ALU.subtract))
            link(V.tensor_scalar(nlam, nlam, -LAM_INIT, None, ALU.add))
            norm_apply(1, memx, xn, True)

            def rope1(u):
                v = u.rearrange("p t (m c) -> p t m c", c=HD)
                x1, x2 = v[:, :, :, 0:8], v[:, :, :, 8:16]
                tmp = [rp[:, 128 * i:128 * i + 128].rearrange("p (t m f) -> p t m f", t=NT, m=8) for i in range(4)]
                sc = scs.rearrange("p (s t f) -> p s t f", s=2, t=NT)
                sn = bc(sc[:, 0].unsqueeze(2), [P, NT, 8, 8])
                cs = bc(sc[:, 1].unsqueeze(2), [P, NT, 8, 8])
                link(V.tensor_tensor(tmp[0], x1, cs, ALU.mult))
                link(V.tensor_tensor(tmp[1], x2, sn, ALU.mult))
                link(V.tensor_tensor(tmp[2], x2, cs, ALU.mult))
                link(V.tensor_tensor(tmp[3], x1, sn, ALU.mult))
                link(V.tensor_tensor(x1, tmp[0], tmp[1], ALU.subtract))
                V.tensor_tensor(x2, tmp[2], tmp[3], ALU.add).then_inc(qk_ready, 1)

            evac(0, u_qa)
            dve.wait_ge(rope_sin, 1)
            rope1(u_qa)
            evac(1, u_ka)
            fill_lo()
            dve.wait_ge(qk_ready, 1)
            rope1(u_ka)
            evac(2, u_va)
            evac(3, qsT, 0.125)
            for x, dst, scale in ((0, qaT, 0.125), (1, kaT, 1.0)):
                for b in range(2):
                    tb_take(lambda src: V.tensor_scalar(dst[:, 512 * b:512 * b + 512], src, scale, None, ALU.mult))
            evac(4, ksT)
            evac(5, u_vs)

            def unit_loop(n0, n1, post, hook):
                for i in range(n0, n1 + 2):
                    if i < n1:
                        u = units[i]
                        dve.wait_ge(sc_done, i + 1)
                        src = bank(4 + i % 2).rearrange("p (s w) -> p s w", w=u["w"])
                        V.tensor_reduce(den_of(i)[1], src, AX.X, ALU.max, negate=True).then_inc(mx_done, 1)
                    if n0 <= i - 1 < n1:
                        dve.wait_ge(tr_done, i)
                        if i - 1 >= 2:
                            dve.wait_ge(pv_done, i - 2)
                        V.tensor_copy(units[i - 1]["pr"][2 + (i - 1) % 2], bank(6)).then_inc(pt_done, 1)
                    if i - 2 >= n0:
                        dve.wait_ge(pv_done, i - 1)
                        post(i - 2, units[i - 2])
                    hook(i)

            def post_diff(n, u):
                k = len(u["segs"])
                nh = k // 2
                link(V.reciprocal(coef[:, 0:k], den_of(n)[0]))
                cv = coef[:, 0:k].rearrange("p (h c) -> p h c", c=2)
                link(V.tensor_scalar(cv[:, :, 1], cv[:, :, 1], nlam, None, ALU.mult))
                o = bank(7)[:, 0:P * k].rearrange("p (s c) -> p s c", c=P)
                w = comb1[:, 0:P * k]
                V.tensor_tensor(w.rearrange("p (s c) -> p s c", c=P), o,
                                bc(coef[:, 0:k].unsqueeze(2), [P, k, P]), ALU.mult).then_inc(post_done, 1)
                dve.wait_ge(post_done, n + 1)
                wv = w.rearrange("p (h c d) -> p h c d", c=2, d=P)
                y = xn[:, u["t"], P * u["hs"][0]:P * u["hs"][0] + P * nh].rearrange("p (h d) -> p h d", d=P)
                link(V.tensor_tensor(y, wv[:, :, 0, :], wv[:, :, 1, :], ALU.add))

            def hook_diff(i):
                if i == 1:
                    evac(6, kmT[:, 0:1024])
                if i == 5:
                    evac(7, kmT[:, 1024:2048])

            dve.wait_ge(tb_done, 8)
            unit_loop(0, U_X, post_diff, hook_diff)
            ya = xn[:, :, 0:512]
            link(V.tensor_tensor(sq1.rearrange("p (t c) -> p t c", t=NT), ya, ya, ALU.mult))
            V.tensor_reduce(ss_s, sq1.rearrange("p (s c) -> p s c", c=P), AX.X, ALU.add).then_inc(sub_sq, 1)
            dve.wait_ge(sub_y0, 1)
            newton(rs_s, ss_s, y0_s, P)
            yv = ya.rearrange("p t (h c) -> p t h c", c=P)
            rv = rs_s.rearrange("p (t h) -> p t h", t=NT)
            link(V.tensor_tensor(yv, yv, bc(rv.unsqueeze(3), [P, NT, 4, P]), ALU.mult))
            link(V.tensor_tensor(yv, yv, bc(gsub.unsqueeze(1).unsqueeze(1), [P, NT, 4, P]), ALU.mult))
            for half in range(2):
                for j in (2 * half, 2 * half + 1):
                    dve.wait_ge(z_ln, j + 1)
                    V.scalar_tensor_tensor(sbz[j % 2], bank(4 + 2 * (j % 2), 2)[:, 0:768], 0.0, sbz[j % 2],
                                           ALU.max, ALU.add).then_inc(z_sp, 1)
                evac(8 + half, vm[:, :, 512 * half:512 * half + 512])
            dve.wait_ge(z_pv, 4)
            V.tensor_copy(xn[:, :, 512:1024], bank(2, 2).rearrange("p (t c) -> p t c", t=NT)).then_inc(xn_ready, 2)
            fill_lo()
            residual(11, src_ready)
            norm_apply(2, h, xn, True)
            fill_lo()
            evac(12, qxT[:, 0:1024], 0.0625)
            evac(13, qxT[:, 1024:2048], 0.0625)

            def post_cross(n, u):
                k = 2
                link(V.reciprocal(coef[:, 0:k], den_of(n)[0]))
                o = bank(7).rearrange("p (s c) -> p s c", c=256)
                y = xn[:, u["t"], 256 * u["hs"][0]:256 * u["hs"][0] + 512].rearrange("p (s c) -> p s c", c=256)
                V.tensor_tensor(y, o, bc(coef[:, 0:k].unsqueeze(2), [P, k, 256]), ALU.mult).then_inc(post_done, 1)
                dve.wait_ge(post_done, n + 1)

            unit_loop(U_X, U_A, post_cross, lambda i: None)
            signal(xn_ready, 2)
            fill_lo()
            residual(15, src_ready)
            norm_apply(3, h, xn, True)
            fill_lo()

            def mlp(base, a0, abuf, before):
                for j in range(8):
                    dve.wait_ge(strip_done, up_strip(base, j) + 1)
                    V.tensor_scalar(act_q, bank(4 + 2 * (j % 2), 2), 0.0, None, ALU.max).then_inc(up_evac, 1)
                    dve.wait_ge(up_evac, a0 + j + 1)
                    V.tensor_tensor(act_q, act_q, act_q, ALU.mult).then_inc(sq_ready, 1)
                    dve.wait_ge(sq_ready, a0 + j + 1)
                    dve.wait_ge(a_hi, a0 + j + 1)
                    c = slice(1024 * (j % 2), 1024 * (j % 2) + 1024)
                    V.tensor_tensor(XL[abuf][:, c], act_q, XH[abuf][:, c].bitcast(f32),
                                    ALU.subtract).then_inc(a_lo, 1)
                    dve.wait_ge(a_lo, a0 + j + 1)

            mlp(MLP1, 0, 0, MLP1)
            residual(IN2 - 1, src_ready)
            norm_apply(4, h, h, False)
            signal(src_ready, 1)
            norm_apply(5, h, xn, True)
            fill_lo()
            dve.wait_ge(tb_done, tb[0])

            cs2 = cst[:, C_CS2:C_CS2 + 64].rearrange("p (t f) -> p t f", t=NT)
            sn2 = cst[:, C_SN2:C_SN2 + 64].rearrange("p (t f) -> p t f", t=NT)

            def head_norm(i, col, heads, gain, outs):
                g = gq[:, 64 * gain:64 * gain + 64]
                t1 = T1.rearrange("p (t h f) -> p t h f", t=NT, h=2)
                t2 = T2.rearrange("p (t h f) -> p t h f", t=NT, h=2)
                link(V.tensor_tensor(t1, bc(cs2.unsqueeze(2), [P, NT, 2, 32]),
                                     bc(g.rearrange("p (h f) -> p h f", h=2).unsqueeze(1), [P, NT, 2, 32]), ALU.mult))
                link(V.scalar_tensor_tensor(t2[:, :, 0], sn2, -1.0, bc(g[:, 32:64].unsqueeze(1), [P, NT, 32]),
                                            ALU.mult, ALU.mult))
                link(V.tensor_tensor(t2[:, :, 1], sn2, bc(g[:, 0:32].unsqueeze(1), [P, NT, 32]), ALU.mult))
                x = u2[:, :, col:col + 64 * heads].rearrange("p t (m c) -> p t m c", c=HD)
                n = 128 * heads
                va = ta[:, 0:n].rearrange("p (t m c) -> p t m c", t=NT, c=HD)
                vb = sqb[:, 0:n].rearrange("p (t m c) -> p t m c", t=NT, c=HD)
                link(V.tensor_tensor(va, x, bc(T1.rearrange("p (t c) -> p t c", t=NT).unsqueeze(2),
                                               [P, NT, heads, HD]), ALU.mult))
                dve.wait_ge(hn_sq, i + 1)
                V.tensor_reduce(ss_h[:, 0:2 * heads], sqb[:, 0:n].rearrange("p (s c) -> p s c", c=HD),
                                AX.X, ALU.add).then_inc(hn_ss, 1)
                dve.wait_ge(hn_ss, i + 1)
                t2c = T2.rearrange("p (t c) -> p t c", t=NT)
                for z in range(2):
                    link(V.tensor_tensor(vb[:, :, :, 32 * z:32 * z + 32], x[:, :, :, 32 - 32 * z:64 - 32 * z],
                                         bc(t2c[:, :, 32 * z:32 * z + 32].unsqueeze(2), [P, NT, heads, 32]), ALU.mult))
                link(V.tensor_tensor(va, va, vb, ALU.add))
                dve.wait_ge(hn_y0, i + 1)
                newton(rs_h[:, 0:2 * heads], ss_h[:, 0:2 * heads], y0_h[:, 0:2 * heads], HD)
                r = bc(rs_h[:, 0:2 * heads].rearrange("p (t m) -> p t m", t=NT).unsqueeze(3), [P, NT, heads, HD])
                for o in outs:
                    link(V.tensor_tensor(o, va, r, ALU.mult))
                signal(hn_done, 1)

            def u2_evac(c):
                evac(IN2 + c, u2[:, :, 512 * c:512 * c + strips[IN2 + c]["w"]])

            def dup_views(buf):
                v = buf.rearrange("p (t g d c) -> p t g d c", t=NT, g=3, d=2)
                return [v[:, :, :, 0, :], v[:, :, :, 1, :]]

            u2_evac(0)
            u2_evac(1)
            x = u2[:, :, QA:QA + 768].rearrange("p t (m c) -> p t m c", c=HD)
            head_norm(0, QA, 12, 0, [x])
            u2_evac(2)
            u2_evac(3)
            head_norm(1, KS, 3, 1, dup_views(kdup[0]))
            head_norm(2, KW, 3, 2, dup_views(kdup[1]))
            for b in range(3):
                tb_take(lambda src: V.tensor_scalar(qT[:, 512 * b:512 * b + 512], src, 0.125, None, ALU.mult))
            u2_evac(4)
            for kv, col in ((0, KC), (1, VC)):
                for o in dup_views(cdup[:, 768 * kv:768 * kv + 768]):
                    link(V.tensor_copy(o, u2[:, :, col:col + 192].rearrange("p t (g c) -> p t g c", g=3)))
            signal(at_ready, 1)
            for b in range(3):
                tb_take(lambda src: V.tensor_copy(kT[:, 512 * b:512 * b + 512], src))
            u2_evac(5)
            x = u2[:, :, QB:QB + 768].rearrange("p t (m c) -> p t m c", c=HD)
            head_norm(3, QB, 12, 3, [x])
            tb_take(lambda src: V.tensor_copy(pe2, src[:, 0:32]))
            for b in range(3):
                dve.wait_ge(tb_done, tb[0] + 1)
                src = bank(4 + tb[0] % 4)
                link(V.tensor_copy(kc2[0:64, 512 * b:512 * b + 512], src[0:64, :]))
                V.tensor_copy(kc2[64:128, 512 * b:512 * b + 512].rearrange("p (g u) -> p g u", u=S)[:, :, 0:S - 1],
                              src[64:128, :].rearrange("p (g u) -> p g u", u=S)[:, :, 1:S]).then_inc(tb_evac, 1)
                tb[0] += 1
                dve.wait_ge(tb_evac, tb[0])
            for kv in range(2):
                at = AT[:, 720 * kv:720 * kv + 720].rearrange("p (y g c) -> p y g c", y=16, g=3)
                src = kc2[:, 768 * kv:768 * kv + 768].rearrange("p (g c y z) -> p y g c z", g=3, y=8, z=2)
                for th in range(2):
                    pe = pe2[:, 16 * kv + 8 * th:16 * kv + 8 * th + 8]
                    link(V.tensor_tensor(at[:, 8 * th:8 * th + 8], src[:, :, :, th:th + CMP_N, 0],
                                         bc(pe.unsqueeze(2).unsqueeze(2), [P, 8, 3, CMP_N]), ALU.add))
            signal(at_ready, 1)
            u2_evac(6)
            head_norm(4, KB, 12, 4, [u2[:, :, KB:KB + 768].rearrange("p t (m c) -> p t m c", c=HD)])
            tb_take(lambda src: V.tensor_copy(hx, src[:, 0:180]))
            link(V.tensor_tensor(hg, hx, hx, ALU.mult))
            link(V.tensor_scalar(hg, hg, 0.044715, 1.0, ALU.mult, ALU.add))
            link(V.tensor_tensor(hg, hg, hx, ALU.mult))
            V.tensor_scalar(hu, hg, -2.0 * math.sqrt(2.0 / math.pi), 80.0, ALU.mult, ALU.min).then_inc(ge_arg, 1)
            dve.wait_ge(ge_exp, 1)
            link(V.tensor_scalar(hu, hu, 1.0, None, ALU.add))
            link(V.reciprocal(hu, hu))
            V.tensor_tensor(hx, hx, hu, ALU.mult).then_inc(hid_ready, 1)
            u2_evac(7)
            u2_evac(8)
            gv = sgn.rearrange("p (t c) -> p t c", t=NT)
            V.tensor_scalar(gv, u2[:, :, GA:GA + 36], -80.0, None, ALU.max).then_inc(sg_arg, 1)
            dve.wait_ge(tb_done, tb[0] + 1)
            src = bank(4 + tb[0] % 4)
            link(V.tensor_copy(kcn, src[0:15, 0:192]))
            for i in range(3):
                link(V.tensor_copy(vcr[32 * i:32 * i + 15, :], src[32 * i:32 * i + 15, 256:448]))
            V.tensor_copy(vcr[96:111, :], src[96:111, 256:448]).then_inc(tb_evac, 1)
            tb[0] += 1
            dve.wait_ge(tb_evac, tb[0])
            kt_ = ktmp[0:15, :]
            link(V.tensor_tensor(kt_, kcn, kcn, ALU.mult))
            V.tensor_reduce(ss_h[0:15, 0:3], kt_.rearrange("p (g c) -> p g c", g=3), AX.X, ALU.add).then_inc(kc_ss, 1)
            dve.wait_ge(kc_y0, 1)
            newton(rs_h[0:15, 0:3], ss_h[0:15, 0:3], y0_h[0:15, 0:3], HD)
            k3 = kcn.rearrange("p (g c) -> p g c", g=3)
            link(V.tensor_tensor(k3, k3, bc(rs_h[0:15, 0:3].unsqueeze(2), [15, 3, HD]), ALU.mult))
            link(V.tensor_tensor(k3, k3, bc(gq[0:15, 320:384].unsqueeze(1), [15, 3, HD]), ALU.mult))
            kd = kcd.rearrange("p (g d c) -> p g d c", g=3, d=2)
            t3 = kt_.rearrange("p (g c) -> p g c", g=3)
            cc, sn = cst[0:15, C_KCC:C_KCC + 32], cst[0:15, C_KCS:C_KCS + 32]
            for z in range(2):
                mine, other = k3[:, :, 32 * z:32 * z + 32], k3[:, :, 32 - 32 * z:64 - 32 * z]
                link(V.tensor_tensor(t3[:, :, 0:32], mine, bc(cc.unsqueeze(1), [15, 3, 32]), ALU.mult))
                link(V.tensor_tensor(t3[:, :, 32:64], other, bc(sn.unsqueeze(1), [15, 3, 32]), ALU.mult))
                for d in range(2):
                    link(V.tensor_tensor(kd[:, :, d, 32 * z:32 * z + 32], t3[:, :, 0:32], t3[:, :, 32:64],
                                         ALU.add if z else ALU.subtract))
            signal(kc_ready, 1)
            dve.wait_ge(sg_exp, 1)
            link(V.tensor_scalar(sgn, sgn, 1.0, None, ALU.add))
            link(V.reciprocal(sgn, sgn))
            tb_take(lambda src: V.tensor_copy(kcT[:, :], src[:, 0:48]))
            signal(kc_ready, 1)
            s4 = scb[:, :].rearrange("p (t m c) -> p t m c", t=NT, m=12)
            s3 = scb[:, :].rearrange("p (s c) -> p s c", c=CMP_N)
            cma = cst[:, C_CMA:C_CMA + 30].rearrange("p (t c) -> p t c", t=NT)
            cmm = cst[:, C_CMM:C_CMM + 30].rearrange("p (t c) -> p t c", t=NT)
            tb_take(lambda src: V.tensor_tensor(
                s4, src[:, 0:384].rearrange("p (t m c) -> p t m c", t=NT, m=12)[:, :, :, 0:15],
                bc(cma.unsqueeze(2), [P, NT, 12, CMP_N]), ALU.add))
            link(V.tensor_reduce(smax, s3, AX.X, ALU.max))
            V.tensor_tensor(s3, s3, bc(smax.unsqueeze(2), [P, 24, CMP_N]), ALU.subtract).then_inc(cs_arg, 1)
            link(V.memset(pc, 0.0))
            dve.wait_ge(cs_exp, 1)
            link(V.tensor_reduce(cden, s3, AX.X, ALU.add))
            link(V.reciprocal(cden, cden))
            g4 = sgn.rearrange("p (t m b) -> p t m b", t=NT, b=3)
            c3 = cden.rearrange("p (t m) -> p t m", t=NT)
            link(V.tensor_tensor(c3, c3, g4[:, :, :, 0], ALU.mult))
            link(V.tensor_tensor(s4, s4, bc(cmm.unsqueeze(2), [P, NT, 12, CMP_N]), ALU.mult))
            V.tensor_tensor(pc.rearrange("p (s c) -> p s c", c=32)[:, :, 0:15], s3,
                            bc(cden.unsqueeze(2), [P, 24, CMP_N]), ALU.mult).then_inc(pc_ready, 1)
            tb_take(lambda src: V.tensor_copy(pcT[:, 0:512], src))
            tb_take(lambda src: V.tensor_copy(pcT[:, 512:768], src[:, 0:256]))
            signal(pc_ready, 1)
            xf = xn[:, :, :].rearrange("p t c -> p (t c)")
            for b in range(3):
                t, c = divmod(512 * b, 768)
                if c + 512 <= 768:
                    tb_take(lambda src: V.tensor_copy(xn[:, t, c:c + 512], src))
                else:
                    dve.wait_ge(tb_done, tb[0] + 1)
                    src = bank(4 + tb[0] % 4)
                    link(V.tensor_copy(xn[:, t, c:768], src[:, 0:768 - c]))
                    V.tensor_copy(xn[:, t + 1, 0:c + 512 - 768], src[:, 768 - c:512]).then_inc(tb_evac, 1)
                    tb[0] += 1
                    dve.wait_ge(tb_evac, tb[0])
            for b in range(3):
                tb_take(lambda src: V.tensor_scalar(qbT[:, 512 * b:512 * b + 512], src, 0.125, None, ALU.mult))
            for b in range(3):
                tb_take(lambda src: V.tensor_copy(kbT[:, 512 * b:512 * b + 512], src))

            def post_nsa(n, u):
                k = len(u["segs"])
                nh = k // 2
                t, h0 = u["t"], u["hs"][0]
                link(V.reciprocal(coef[:, 0:k], den_of(n)[0]))
                cv = coef[:, 0:k].rearrange("p (m b) -> p m b", b=2)
                link(V.tensor_tensor(cv, cv, g4[:, t, h0:h0 + nh, 1:3], ALU.mult))
                w = comb2[:, 0:64 * k]
                V.tensor_tensor(w.rearrange("p (s c) -> p s c", c=64),
                                bank(7)[:, 0:64 * k].rearrange("p (s c) -> p s c", c=64),
                                bc(coef[:, 0:k].unsqueeze(2), [P, k, 64]), ALU.mult).then_inc(post_done, 1)
                dve.wait_ge(post_done, n + 1)
                wv = w.rearrange("p (m b c) -> p m b c", b=2, c=64)
                y = xn[:, t, 64 * h0:64 * h0 + 64 * nh].rearrange("p (m c) -> p m c", c=64)
                link(V.tensor_tensor(y, y, wv[:, :, 0], ALU.add))
                link(V.tensor_tensor(y, y, wv[:, :, 1], ALU.add))

            def post_dil(n, u):
                k = len(u["segs"])
                c = 512 + 64 * u["hs"][0]
                V.tensor_copy(u2[:, u["t"], c:c + 64 * k], bank(7)[:, 0:64 * k]).then_inc(post_done, 1)

            gate_cols = [QB, QB + 512, QB + 1024, QA]

            def hook2(i):
                for g in range(4):
                    if i == U_A + GATE_STEP[g]:
                        s = IN2 + 9 + g
                        dve.wait_ge(strip_done, s + 1)
                        src = bank(strips[s]["pair"], 2).rearrange("p (t c) -> p t c", t=NT)
                        V.tensor_copy(u2[:, :, gate_cols[g]:gate_cols[g] + 512], src).then_inc(evac_done, 1)
                        dve.wait_ge(evac_done, strips[s]["evac"])
                        signal(gates_in, 1)

            unit_loop(U_A, NU, lambda n, u: (post_nsa if u["kind"] == "nsa" else post_dil)(n, u), hook2)
            dve.wait_ge(post_done, NU)
            signal(dl_den, 1)
            link(V.reciprocal(dl[2], dil_den))
            dve.wait_ge(dl_ln, 1)
            link(V.tensor_tensor(dl[1], dl[0], dil_nm, ALU.subtract))
            lse = dl[1].rearrange("p (t g i) -> p t g i", t=NT, g=3)
            d8v = [x.rearrange("p (t i) -> p t i", t=NT) for x in d8]
            link(V.tensor_reduce(d8v[0], lse.rearrange("p t g i -> p t i g"), AX.X, ALU.max))
            V.tensor_tensor(lse, lse, bc(d8v[0].unsqueeze(2), [P, NT, 3, 4]), ALU.subtract).then_inc(dl_arg, 1)
            dve.wait_ge(dl_exp, 1)
            link(V.tensor_reduce(d8v[1], lse.rearrange("p t g i -> p t i g"), AX.X, ALU.add))
            link(V.reciprocal(d8[2], d8[1]))
            link(V.tensor_tensor(dl[1], dl[1], dl[2], ALU.mult))
            link(V.tensor_tensor(lse, lse, bc(d8v[2].unsqueeze(2), [P, NT, 3, 4]), ALU.mult))
            for t in range(NT):
                o = u2[:, t, 512:1280].rearrange("p (s c) -> p s c", c=64)
                link(V.tensor_tensor(o, o, bc(dl[1][:, 12 * t:12 * t + 12].unsqueeze(2), [P, 12, 64]), ALU.mult))
                link(V.tensor_tensor(u2[:, t, 512:768], u2[:, t, 512:768], u2[:, t, 768:1024], ALU.add))
                V.tensor_tensor(xn[:, t, 768:1024], u2[:, t, 512:768], u2[:, t, 1024:1280],
                                ALU.add).then_inc(xn_ready, 1)
            fill_lo()
            dve.wait_ge(gates_sig, 2)
            dve.wait_ge(strip_done, IN2 + 15)
            for t in range(NT):
                for n in range(2):
                    b = 2 * t + n
                    link(V.tensor_tensor(xn[:, t, 512 * n:512 * n + 512], bank(b),
                                         u2[:, t, gate_cols[n]:gate_cols[n] + 512], ALU.mult))
                    gb = u2[:, t, gate_cols[2 + n]:gate_cols[2 + n] + 512]
                    link(V.tensor_tensor(gb, bank(4 + b), gb, ALU.mult))
                    x = V.tensor_tensor(xn[:, t, 512 * n:512 * n + 512], xn[:, t, 512 * n:512 * n + 512], gb, ALU.add)
                    if n == 0:
                        link(x)
                    else:
                        x.then_inc(xn_ready, 1)
            signal(evac_done, 1)
            fill_lo()
            residual(IN2 + 16, src_ready)
            norm_apply(6, h, xn, True)
            fill_lo()
            mlp(MLP2, 8, 1, MLP2)
            residual(NS - 1, res_done)

        @block.tensor
        def _(pe):
            T = nc.tensor
            tb = [0]
            ups = [0]
            fills = [0]
            a_n = [0]
            row_n = [0]

            def switch_rows(last):
                row_n[0] += 1
                last.then_inc(row_step, 1)
                pe.wait_ge(row_step, row_n[0])

            def three(dst, xh, xl, wh, wl, start, stop, w_stationary):
                pairs = [(xh, wh), (xh, wl), (xl, wh)] if not w_stationary else [(xh, wh), (xl, wh), (xh, wl)]
                for i, (x, w) in enumerate(pairs):
                    l, r = (w, x) if w_stationary else (x, w)
                    last = T.matmul(dst, l, r, start=start and i == 0, stop=stop and i == 2)
                return last

            def strip(s):
                d = strips[s]
                m = d["mode"]
                hi_, lo_ = HI[s % 2], LO[s % 2]
                xh, xl = XH[d["x"]], XL[d["x"]]
                pe.wait_ge(lo_done, split_before[half_of[s][-1]] + 1)
                if m == "up":
                    if d["j"] >= 2 or ups[0] >= 8:
                        pe.wait_ge(up_evac, ups[0] - 1)
                    b0 = 4 + 2 * (d["j"] % 2)
                    ups[0] += 1
                else:
                    if d["need_evac"]:
                        pe.wait_ge(evac_done, d["need_evac"])
                    b0 = d.get("pair", 0)
                w = d["w"]
                if m == "tok":
                    for t in range(NT):
                        for k in range(KT):
                            c = 2048 * (k // 4) + w * (k % 4)
                            x0 = S * k + P * t
                            last = three(bank(b0 + t)[:, 0:w], xh[:, x0:x0 + P], xl[:, x0:x0 + P],
                                         hi_[:, c:c + w], lo_[:, c:c + w], k == 0, k == KT - 1, False)
                elif m in ("T", "up"):
                    for c4 in range(4):
                        for k in range(KT):
                            c = 2048 * (k // 4) + w * (k % 4) + P * c4
                            dst = PS[:, 512 * b0 + S * c4:512 * b0 + S * c4 + S]
                            last = three(dst, xh[:, S * k:S * k + S], xl[:, S * k:S * k + S],
                                         hi_[:, c:c + P], lo_[:, c:c + P], k == 0, k == KT - 1, True)
                else:
                    if m == "down":
                        a_n[0] += 1
                        pe.wait_ge(a_lo, a_n[0])
                    for t in range(NT):
                        for n in range(2):
                            for k in range(4):
                                c = 1024 * k + 512 * n
                                x0 = S * (d["k0"] + k) + P * t
                                b = 2 * t + n
                                start, stop = d["first"] and k == 0, d["last"] and k == 3
                                if m == "mixed":
                                    start, stop = k == 2, k in (1, 3)
                                    b += 4 * (k // 2)
                                last = three(bank(b), xh[:, x0:x0 + P], xl[:, x0:x0 + P],
                                             hi_[:, c:c + 512], lo_[:, c:c + 512], start, stop, False)
                last.then_inc(strip_done, 1)

            def tb_bank():
                n = tb[0]
                if n >= 4:
                    pe.wait_ge(tb_evac, n - 3)
                tb[0] += 1
                return bank(4 + n % 4)

            def fill(k):
                for b in range(4):
                    t, kh = b // 2, b % 2
                    pe.wait_ge(xn_ready, 2 * fills[0] + t + 1)
                    dst = tb_bank()
                    for q in range(4):
                        c = P * (4 * kh + q)
                        last = T.transpose(dst[:, P * q:P * q + P], xn[:, t, c:c + P], ident)
                    last.then_inc(tb_done, 1)
                fills[0] += 1

            def head_T(src, n_pairs):
                for b in range(n_pairs // 2):
                    dst = tb_bank()
                    for q in range(4):
                        pair, t = 2 * b + q // 2, q % 2
                        last = T.transpose(dst[:, P * q:P * q + P], src(pair, t), ident)
                    last.then_inc(tb_done, 1)

            def unit_loop(n0, n1, hook):
                for i in range(n0, n1 + 2):
                    if i < n1:
                        u = units[i]
                        if i >= 2:
                            pe.wait_ge(ex_done, i - 1)
                        rows = None
                        for si, sg in sorted(enumerate(u["segs"]), key=lambda e: e[1]["row"]):
                            if rows is not None and sg["row"] != rows:
                                switch_rows(last)
                            rows = sg["row"]
                            dst = bank(4 + i % 2)[:, u["w"] * si:u["w"] * si + u["w"]]
                            nq = len(sg["qk"])
                            for x, (q, k) in enumerate(sg["qk"]):
                                last = T.matmul(dst, q, k, start=x == 0, stop=x == nq - 1 and not sg["mask"])
                            for c, m in sg["mask"]:
                                last = T.matmul(dst[:, c:c + m.shape[1]], identb, m, start=False, stop=True)
                        last.then_inc(sc_done, 1)
                    if n0 <= i - 1 < n1:
                        pe.wait_ge(ex_done, i)
                        if i - 1 >= 1:
                            pe.wait_ge(pt_done, i - 1)
                        for q in range(4):
                            last = T.transpose(bank(6)[:, P * q:P * q + P],
                                               units[i - 1]["pr"][(i - 1) % 2][:, P * q:P * q + P], ident)
                        last.then_inc(tr_done, 1)
                    if i - 2 >= n0:
                        n = i - 2
                        u = units[n]
                        pe.wait_ge(pt_done, n + 1)
                        if n >= 1:
                            pe.wait_ge(post_done, n)
                        pt = u["pr"][2 + n % 2]
                        nk = u["w"] // P
                        for si, sg in enumerate(u["segs"]):
                            for k in range(nk):
                                c = u["w"] * si + P * k
                                last = T.matmul(bank(7)[:, sg["vw"] * si:sg["vw"] * si + sg["vw"]],
                                                pt[:, c:c + P], sg["v"][k], start=k == 0, stop=k == nk - 1)
                        last.then_inc(pv_done, 1)
                    hook(i)

            pe.wait_ge(cst_loaded, 16)
            fill(0)
            pe.wait_ge(tb_evac, tb[0])
            strip(0)
            strip(1)
            fill(1)
            strip(2)
            strip(3)
            pe.wait_ge(qk_ready, 2)
            for u in (u_qa, u_ka):
                head_T(lambda pair, t: u[:, t, P * pair:P * pair + P], 4)
            strip(4)
            strip(5)
            pe.wait_ge(masks_ready, 2)
            pe.wait_ge(tb_evac, tb[0])
            pe.wait_ge(evac_done, 6)

            def hook1(i):
                if i == 1:
                    strip(6)
                if i == 5:
                    strip(7)

            unit_loop(0, U_X, hook1)

            def z_scores(j):
                if j >= 2:
                    pe.wait_ge(z_at, j - 1)
                b = bank(4 + 2 * (j % 2), 2)
                for hh in range(2):
                    if hh:
                        switch_rows(last)
                    r = slice(64 * hh, 64 * hh + 64)
                    for kt in range(2):
                        w = S - P * kt
                        c = 512 * kt + w * hh
                        T.matmul(b[:, c:c + w], ksT[r, S * j + P * kt:S * j + P * kt + P],
                                 qsT[r, S * j + P * kt:S * j + S], start=hh == 0, stop=True, skip_group_check=True)
                        last = T.matmul(b[:, c:c + P], identb, maskb(C_STR, P), start=False, stop=True,
                                        skip_group_check=True)
                last.then_inc(z_done, 1)

            def z_sums(j):
                pe.wait_ge(z_sp, j + 1)
                b, sp = bank(4 + 2 * (j % 2), 2), sbz[j % 2]
                for hh in range(2):
                    T.matmul(b[:, S * hh:S * hh + S], tri, sp[:, S * hh:S * hh + S], start=False, stop=True,
                             skip_group_check=True)
                    T.matmul(b[:, S * hh + P:S * hh + S], negones, sp[:, 512 + P * hh:512 + P * hh + P],
                             start=False, stop=True, skip_group_check=True)
                    last = T.matmul(b[:, 512 + P * hh:512 + P * hh + P], tri, sp[:, 512 + P * hh:512 + P * hh + P],
                                    start=False, stop=True, skip_group_check=True)
                last.then_inc(z_cum, 1)

            def z_out(j):
                pe.wait_ge(z_at, j + 1)
                w = sba[j % 2]
                for hh in range(2):
                    c = 64 * (2 * j + hh)
                    T.matmul(bank(2)[:, c:c + 64], w[:, S * hh:S * hh + P], u_vs[:, 0, c:c + 64], start=True, stop=True)
                    T.matmul(bank(3)[:, c:c + 64], w[:, S * hh + P:S * hh + S], u_vs[:, 0, c:c + 64],
                             start=True, stop=False)
                    last = T.matmul(bank(3)[:, c:c + 64], w[:, 512 + P * hh:512 + P * hh + P],
                                    u_vs[:, 1, c:c + 64], start=False, stop=True)
                last.then_inc(z_pv, 1)

            pe.wait_ge(post_done, U_X)
            for half in range(2):
                z_scores(2 * half)
                z_scores(2 * half + 1)
                strip(8 + half)
                z_sums(2 * half)
                z_sums(2 * half + 1)
                z_out(2 * half)
                z_out(2 * half + 1)
            fill(2)
            for s in (10, 11):
                pe.wait_ge(tb_evac, tb[0])
                strip(s)
            fill(3)
            pe.wait_ge(tb_evac, tb[0])
            strip(12)
            strip(13)
            pe.wait_ge(evac_done, strips[13]["evac"])
            unit_loop(U_X, U_A, lambda i: None)
            pe.wait_ge(post_done, U_A)
            fill(4)
            pe.wait_ge(tb_evac, tb[0])
            strip(14)
            strip(15)
            fill(5)
            pe.wait_ge(tb_evac, tb[0])
            for s in range(MLP1, IN2):
                strip(s)
            pe.wait_ge(up_evac, 8)
            fill(6)
            pe.wait_ge(tb_evac, tb[0])
            for c in range(4):
                strip(IN2 + c)
            pe.wait_ge(hn_done, 1)
            head_T(lambda pair, t: u2[:, t, QA + P * pair:QA + P * pair + P], 6)
            strip(IN2 + 4)
            pe.wait_ge(hn_done, 3)
            kd = [b.rearrange("p (t g c) -> p t g c", t=NT, g=3) for b in kdup]
            head_T(lambda pair, t: kd[pair // 3][:, t, pair % 3, :], 6)
            strip(IN2 + 5)
            dst = tb_bank()
            pe.wait_ge(misc_loaded, 16 * 16)
            T.transpose(dst[:, 0:32], vecs[0:32, :], ident[0:32, 0:32]).then_inc(tb_done, 1)
            pe.wait_ge(at_ready, 1)
            cd = [cdup[:, 768 * i:768 * i + 768].rearrange("p (t g c) -> p t g c", t=NT, g=3) for i in range(2)]
            head_T(lambda pair, t: cd[pair // 3][:, t, pair % 3, :], 6)
            strip(IN2 + 6)
            pe.wait_ge(at_ready, 2)
            dst = tb_bank()
            for kv in range(2):
                for q in range(2):
                    raw_wait(pe, raw_halves[2 * kv + q])
                for half in range(2):
                    o = dst[:, 90 * kv + 45 * half:90 * kv + 45 * half + 45]
                    for k in range(16):
                        wgt = RAW[raw_halves[2 * kv + k // 8] % 3]
                        c = 256 * (k % 8) + P * half
                        last = T.matmul(o, wgt[:, c:c + P], AT[:, 720 * kv + 45 * k:720 * kv + 45 * k + 45],
                                        start=k == 0, stop=k == 15)
                last.then_inc(raw_used, 1)
            T.matmul(dst[0:32, 448:449], ident[0:32, 0:32], ident[0:32, 0:1], start=True, stop=True).then_inc(tb_done, 1)
            strip(IN2 + 7)
            strip(IN2 + 8)
            pe.wait_ge(hid_ready, 1)
            dst = tb_bank()
            for kv in range(2):
                for g in range(3):
                    for i in range(1 if kv == 0 else 4):
                        o = dst[32 * i:32 * i + 15, 256 * kv + 64 * g:256 * kv + 64 * g + 64]
                        for half in range(2):
                            c = 90 * kv + 45 * half + 15 * g
                            last = T.matmul(o, hx[:, c:c + 15], w2sb[:, kv, half, :], start=half == 0, stop=half == 1)
            last.then_inc(tb_done, 1)
            pe.wait_ge(kc_ready, 1)
            dst = tb_bank()
            for g in range(3):
                last = T.transpose(dst[:, 16 * g:16 * g + 15], kcd[:, P * g:P * g + P], ident[0:15, 0:15])
            last.then_inc(tb_done, 1)
            pe.wait_ge(kc_ready, 2)
            dst = tb_bank()
            for odd in range(2):
                if odd:
                    switch_rows(last)
                for hh, t in [(hh, t) for hh in range(odd, 12, 2) for t in range(NT)]:
                    r = slice(64 * (hh % 2), 64 * (hh % 2) + 64)
                    c = 16 * (12 * t + hh)
                    q = qT[r, 256 * (hh // 2) + P * t:256 * (hh // 2) + P * t + P]
                    last = T.matmul(dst[:, c:c + 15], q, kcT[r, 16 * (hh // 4):16 * (hh // 4) + 15],
                                    start=True, stop=True)
            last.then_inc(tb_done, 1)
            pe.wait_ge(pc_ready, 1)
            for lo4, hi4 in ((0, 4), (4, 6)):
                dst = tb_bank()
                for q in range(lo4, hi4):
                    last = T.transpose(dst[:, P * (q - lo4):P * (q - lo4) + P], pc[:, P * q:P * q + P], ident)
                last.then_inc(tb_done, 1)
            pe.wait_ge(pc_ready, 2)
            for b in range(3):
                dst = tb_bank()
                for q in (0, 4, 1, 5, 2, 6, 3, 7):
                    if q in (1, 2, 3):
                        switch_rows(last)
                    t, hh = divmod(8 * b + q, 12)
                    r = slice(32 * (hh % 4), 32 * (hh % 4) + 15)
                    g = hh // 4
                    last = T.matmul(dst[:, 64 * q:64 * q + 64], pcT[r, P * (3 * t + g):P * (3 * t + g) + P],
                                    vcr[r, 64 * g:64 * g + 64], start=True, stop=True)
                last.then_inc(tb_done, 1)
            pe.wait_ge(hn_done, 5)
            head_T(lambda pair, t: u2[:, t, QB + P * pair:QB + P * pair + P], 6)
            head_T(lambda pair, t: u2[:, t, KB + P * pair:KB + P * pair + P], 6)
            pe.wait_ge(tb_evac, tb[0])

            def hook2(i):
                for g in range(4):
                    if i == U_A + GATE_STEP[g]:
                        strip(IN2 + 9 + g)

            unit_loop(U_A, NU, hook2)
            pe.wait_ge(post_done, NU)
            assert tb[0] == TB_Y2, tb[0]
            fill(7)
            pe.wait_ge(tb_evac, tb[0])
            strip(IN2 + 13)
            strip(IN2 + 14)
            pe.wait_ge(evac_done, strips[IN2 + 14]["evac"])
            fill(8)
            pe.wait_ge(tb_evac, tb[0])
            strip(IN2 + 15)
            strip(IN2 + 16)
            fill(9)
            pe.wait_ge(tb_evac, tb[0])
            for s in range(MLP2, NS):
                strip(s)


def _pieces():
    rest, out = 2 * math.pi, []
    for bits in (8, 9, 9):
        e = math.floor(math.log2(rest))
        q = 2.0 ** (e - bits + 1)
        p = math.floor(rest / q) * q
        out.append(p)
        rest -= p
    return out + [float(np.float32(rest))]


TWO_PI = _pieces()
PI_LOW = float(np.nextafter(np.float32(math.pi), np.float32(0)))
GATE_STEP = (1, 7, 13, 19)
TB_Y2 = 57

_INS = ["x", "mem", "positions", "g_mix", "w_in", "lambda_q1", "lambda_k1", "lambda_q2", "lambda_k2",
        "g_subln", "w_out", "g_cross", "g_mem", "w_xq", "w_xkv", "w_xo", "g_mlp", "w_up", "w_down",
        "g_final", "norm1_g_2", "w_in_2", "q_norm_a_2", "k_norm_cmp_2", "k_norm_slc_2", "k_norm_win_2",
        "cmp_k_pos_2", "cmp_k_w1_2", "cmp_k_w2_2", "cmp_v_pos_2", "cmp_v_w1_2", "cmp_v_w2_2",
        "q_norm_b_2", "k_norm_b_2", "w_o_a_2", "w_o_b_2", "w_out_2", "norm2_g_2", "w_up_2", "w_down_2"]


def kernel(**inputs):
    import numpy as _np
    import concourse.bacc as _bacc
    from concourse import mybir as _mybir
    from concourse.bass_utils import run_bass_kernel_spmd as _run

    nc = _bacc.Bacc("TRN2", target_bir_lowering=False, num_devices=1, dynamic_dma_scratch_size=1024)
    arrays, aps = {}, {}
    for name in _INS:
        v = _np.ascontiguousarray(inputs[name])
        arrays[f"in_{name}"] = v
        aps[name] = nc.dram_tensor(f"in_{name}", v.shape, _mybir.dt.from_np(v.dtype), kind="ExternalInput").ap()
    arrays["in_cst"] = constants()
    aps["cst"] = nc.dram_tensor("in_cst", arrays["in_cst"].shape, _mybir.dt.float32, kind="ExternalInput").ap()
    out = nc.dram_tensor("out", (1, S, D), _mybir.dt.float32, kind="ExternalOutput").ap()
    build(nc, aps, out)
    r = _run(nc, [arrays], core_ids=[0])
    return r.results[0]["out"]
```

```python
import math
from contextlib import ExitStack

import numpy as np

import concourse.bass as bass
from concourse import mybir

D = 1024
S = 256
P = 128
NT = S // P
KT = D // P
HD = 64
EPS = 1e-6
NEG = -1e30
FF = 4 * D
CMP_N = (S - 32) // 16 + 1
DIL = ((128, 1), (512, 4), (2048, 16))
QA, KC, VC, KS, VS, KW, VW, GA, QB, KB, VB, GM = (
    0, 768, 960, 1152, 1344, 1536, 1728, 1920, 1956, 2724, 3492, 4260)
LAM_INIT = 0.8 - 0.6 * math.exp(-0.3 * 0)
BIG = 12582912.0

C_ID, C_TRI, C_ONE = 0, 128, 256
C_CS2, C_SN2 = 384, 448
C_CMA, C_CMM = 512, 542
C_KCC, C_KCS = 572, 604
C_INV = 636
C_SMALL = 644
C_CAUS, C_STR, C_DIL = 644, 772, 900
C_ALL = C_DIL + 3 * 384


def constants():
    f = np.float32
    c = np.zeros((P, C_ALL), f)
    i = np.arange(P)
    c[:, C_ID:C_ID + P] = np.eye(P)
    c[:, C_TRI:C_TRI + P] = np.where(i[:, None] >= i[None, :], -1.0, 0.0)
    c[:, C_ONE:C_ONE + P] = -1.0
    inv = np.power(f(10000.0), -np.arange(32, dtype=f) / f(32)).astype(f)
    for t in range(NT):
        ang = (np.arange(t * P, t * P + P, dtype=f)[:, None] * inv[None, :]).astype(f)
        c[:, C_CS2 + 32 * t:C_CS2 + 32 * t + 32] = np.cos(ang)
        c[:, C_SN2 + 32 * t:C_SN2 + 32 * t + 32] = np.sin(ang)
        ok = (16 * np.arange(CMP_N) + 31)[None, :] <= (t * P + i)[:, None]
        c[:, C_CMA + 15 * t:C_CMA + 15 * t + 15] = np.where(ok, 0.0, NEG)
        c[:, C_CMM + 15 * t:C_CMM + 15 * t + 15] = ok
    ang = ((16 * np.arange(CMP_N) + 31).astype(f)[:, None] * inv[None, :]).astype(f)
    c[:CMP_N, C_KCC:C_KCC + 32] = np.cos(ang)
    c[:CMP_N, C_KCS:C_KCS + 32] = np.sin(ang)
    c[:, C_INV:C_INV + 8] = np.power(f(500000.0), -np.arange(0, 16, 2, dtype=f) / f(16))
    c[:, C_CAUS:C_CAUS + P] = np.where(i[None, :] <= i[:, None], 0.0, NEG)
    c[:, C_STR:C_STR + P] = np.where(i[None, :] > i[:, None], 0.0, NEG)
    for g, (win, dil) in enumerate(DIL):
        for t in range(NT):
            d = (t * P + i)[:, None] - np.arange((t + 1) * P)[None, :]
            ok = (d >= 0) & (d % dil == 0) & (d <= win)
            at = C_DIL + 384 * g + P * t
            c[:, at:at + P * (t + 1)] = np.where(ok, 0.0, NEG)
    return c


def build(nc, a, out):
    f32, f32r, bf16, i32 = (mybir.dt.float32, mybir.dt.float32r, mybir.dt.bfloat16, mybir.dt.int32)
    ALU, ACT, AX = mybir.AluOpType, mybir.ActivationFunctionType, mybir.AxisListType
    ctx = ExitStack()
    with ctx:
        def sb(name, shape, dt=f32):
            return ctx.enter_context(nc.sbuf_tensor(name, shape, dt))

        def sem(name):
            return ctx.enter_context(nc.semaphore(name))

        RAW = [sb(f"raw{i}", [P, 2048]) for i in range(3)]
        HI = [sb(f"w_hi{i}", [P, 4096], f32r) for i in range(2)]
        LO = [sb(f"w_lo{i}", [P, 4096], f32r) for i in range(2)]
        XH = [sb(f"x_hi{i}", [P, 2048], f32r) for i in range(2)]
        XL = [sb(f"x_lo{i}", [P, 2048], f32r) for i in range(2)]
        xn = sb("xn", [P, NT, D])
        h = sb("h", [P, NT, D])
        gbuf = [sb(f"gain{i}", [P, D]) for i in range(2)]
        cst = sb("cst", [P, C_SMALL])
        mbf = sb("mbf", [P, P + C_ALL - C_SMALL], bf16)
        AR = sb("arena", [P, 16712])
        ST = sb("small", [P, 1710])
        posi = sb("posi", [P, NT], i32)
        PS = ctx.enter_context(nc.psum_tensor("ps", [P, 4096], f32))

        st_at = [0]

        def small(n):
            st_at[0] += n
            assert st_at[0] <= 1710, st_at[0]
            return ST[:, st_at[0] - n:st_at[0]]

        def bank(b, n=1):
            return PS[:, 512 * b:512 * (b + n)]

        ident = cst[:, C_ID:C_ID + P]
        tri = cst[:, C_TRI:C_TRI + P]
        negones = cst[:, C_ONE:C_ONE + P]
        identb = mbf[:, 0:P]

        def maskb(col, n):
            return mbf[:, P + col - C_SMALL:P + col - C_SMALL + n]

        u_qa, u_ka, u_va, u_vs = (AR[:, 1024 * i:1024 * i + 1024].rearrange("p (t c) -> p t c", t=NT)
                                  for i in range(4))
        qaT, kaT, qsT, ksT = (AR[:, 4096 + 1024 * i:5120 + 1024 * i] for i in range(4))
        kmT = AR[:, 8192:10240]
        vm = AR[:, 10240:12288].rearrange("p (t c) -> p t c", t=NT)
        memx = vm
        pr1 = [AR[:, 12288 + 512 * i:12800 + 512 * i] for i in range(4)]
        sbz = [AR[:, 0:768], AR[:, 14336:15104]]
        sba = [AR[:, 768:1536], AR[:, 15104:15872]]
        comb1 = AR[:, 15872:16384]
        sq1 = AR[:, 12288:13312]
        qxT = AR[:, 0:2048]
        u2 = AR[:, 0:2 * GM].rearrange("p (t c) -> p t c", t=NT)
        qT = AR[:, 8520:10056]
        kT = AR[:, 10056:11592]
        qbT = AR[:, 11592:13128]
        kbT = AR[:, 13128:14664]
        kdup = [AR[:, 11592:12360], AR[:, 12360:13128]]
        cdup = AR[:, 13128:14664]
        kc2 = AR[:, 11592:13128]
        AT = AR[:, 13128:14568]
        pc = AR[:, 11592:12360]
        pcT = AR[:, 12360:13128]
        pr2 = [AR[:, 14664 + 512 * i:15176 + 512 * i] for i in range(4)]
        ta = AR[:, 14664:16200]
        act_q = AR[:, 14664:15688]
        comb2 = gbuf[1][:, 0:256]
        g45 = AR[:, 8520:9544]
        sq_junk = AR[:, 14664:15688]
        sqb = xn[:, :, :].rearrange("p t c -> p (t c)")[:, 0:1536]

        eps = small(1)
        marks = small(40)
        ss_n, y0_n, nr_n = small(14), small(14), small(14)
        t_nr1, t_nr2 = small(48), small(48)
        rstd_n = small(14)
        r45 = small(2)
        rB, diag = AR[:, 15688:15944], AR[:, 15944:16200]
        den, nmx = small(160), small(160)
        coef = small(4)
        lamv = AR[:, 14848:15104]
        lamp = AR[:, 15104:15232]
        lams = small(2)
        lame = small(2)
        nlam = small(1)
        gsub = small(128)
        ss_s, y0_s, rs_s = small(8), small(8), small(8)
        posf = small(2)
        ang = small(32)
        rn = small(32)
        scs = small(32)
        rp = AR[:, 14336:14848]
        gq = small(6 * 64)
        T1, T2 = gbuf[1][:, 256:384], gbuf[1][:, 384:512]
        ss_h, y0_h, rs_h = small(24), small(24), small(24)
        pe2 = small(32)
        vecs = small(128)
        w2sb = sb("w2sb", [P, 2, 2, 64])
        sgn = small(72)
        smax = small(24)
        cden = small(24)
        dl = [small(24) for _ in range(4)]
        d8 = [small(8) for _ in range(3)]
        cwork = gbuf[0][:, :]
        hx, hu, hg = cwork[:, 0:180], cwork[:, 180:360], cwork[:, 360:540]
        kcn = cwork[0:15, 0:192]
        kcd = cwork[0:15, 192:576]
        vcr = cwork[:, 576:768]
        kcT = cwork[:, 768:816]
        ktmp = cwork[:, 816:1008]
        scb = gbuf[1][:, 512:872]

        raw_loaded = [sem(f"raw_loaded{i}") for i in range(3)]
        x_loaded, mem_loaded, cst_loaded = sem("x_loaded"), sem("mem_loaded"), sem("cst_loaded")
        msk_loaded, misc_loaded = sem("msk_loaded"), sem("misc_loaded")
        gain_loaded = [sem(f"gain_loaded{i}") for i in range(7)]
        out_stored = sem("out_stored")
        hi_done = sem("hi_done")
        lo_done = sem("lo_done")
        lo_first = sem("lo_first")
        w1_loaded = sem("w1_loaded")
        raw_used = sem("raw_used")
        strip_done = sem("strip_done")
        evac_done = sem("evac_done")
        tb_done = sem("tb_done")
        tb_hi = sem("tb_hi")
        tb_evac = sem("tb_evac")
        xn_ready = sem("xn_ready")
        norm_sq = sem("norm_sq")
        norm_used = sem("norm_used")
        src_ready = sem("src_ready")
        masks_ready = sem("masks_ready")
        rope_arg = sem("rope_arg")
        rope_sin = sem("rope_sin")
        lam_arg, lam_exp = sem("lam_arg"), sem("lam_exp")
        qk_ready = sem("qk_ready")
        sc_done = sem("sc_done")
        mx_done = sem("mx_done")
        ex_done = sem("ex_done")
        tr_done = sem("tr_done")
        pt_done = sem("pt_done")
        pv_done = sem("pv_done")
        post_done = sem("post_done")
        sub_sq, sub_y0 = sem("sub_sq"), sem("sub_y0")
        z_done, z_ln = sem("z_done"), sem("z_ln")
        z_sp, z_cum, z_at, z_pv = sem("z_sp"), sem("z_cum"), sem("z_at"), sem("z_pv")
        up_evac = sem("up_evac")
        sq_ready = sem("sq_ready")
        a_hi, a_lo = sem("a_hi"), sem("a_lo")
        hn_sq, hn_ss, hn_y0, hn_done = sem("hn_sq"), sem("hn_ss"), sem("hn_y0"), sem("hn_done")
        at_ready, ge_arg, ge_exp, hid_ready = (sem("at_ready"), sem("ge_arg"), sem("ge_exp"),
                                               sem("hid_ready"))
        kc_ss, kc_y0, kc_ready = sem("kc_ss"), sem("kc_y0"), sem("kc_ready")
        sg_arg, sg_exp = sem("sg_arg"), sem("sg_exp")
        cs_arg, cs_exp, pc_ready = sem("cs_arg"), sem("cs_exp"), sem("pc_ready")
        dl_den, dl_ln, dl_arg, dl_exp = sem("dl_den"), sem("dl_ln"), sem("dl_arg"), sem("dl_exp")
        gates_in, gates_sig = sem("gates_in"), sem("gates_sig")
        dl_weights, dl_mixed = sem("dl_weights"), sem("dl_mixed")
        pool_step = sem("pool_step")
        bank_done = sem("bank_done")
        diag_ready = sem("diag_ready")
        rb_done, rb_taken = sem("rb_done"), sem("rb_taken")
        row_step = sem("row_step")
        dve_step = sem("dve_step")
        act_step = sem("act_step")
        res_done = sem("res_done")

        strips, halves = [], []

        def col_strip(w, c0, width, mode, x):
            src = w[0].rearrange("(k p) n -> p k n", p=P)
            strips.append(dict(mode=mode, w=width, x=x))
            for q in range(2):
                halves.append((src[:, 4 * q:4 * q + 4, c0:c0 + width], 4 * width, len(strips) - 1))

        def row_strip(parts, x, k0, first=False, last=False, mode="acc"):
            strips.append(dict(mode=mode, w=D, x=x, k0=k0, first=first, last=last))
            for w, r0 in parts:
                src = w[0, r0:r0 + 2 * P, :].rearrange("(k p) n -> p k n", p=P)
                halves.append((src, 2048, len(strips) - 1))

        def mlp_strips(up, down, x, ax):
            def u(j):
                col_strip(up, 512 * j, 512, "up", x)
                strips[-1]["j"] = j

            def d(j):
                row_strip([(down, 512 * j), (down, 512 * j + 256)], ax, 4 * (j % 2), j == 0, j == 7, "down")
                strips[-1]["j"] = j
            u(0)
            for j in range(1, 8):
                u(j)
                d(j - 1)
            d(7)

        for c, mode in enumerate(("tok", "tok", "tok", "T", "T", "tok")):
            col_strip(a["w_in"], 512 * c, 512, mode, 0)
        for c in range(4):
            col_strip(a["w_xkv"], 512 * c, 512, "T" if c < 2 else "tok", 1)
        for c in range(2):
            row_strip([(a["w_out"], 512 * c), (a["w_out"], 512 * c + 256)], 0, 4 * c, c == 0, c == 1)
        for c in range(2):
            col_strip(a["w_xq"], 512 * c, 512, "T", 1)
        for c in range(2):
            row_strip([(a["w_xo"], 512 * c), (a["w_xo"], 512 * c + 256)], 0, 4 * c, c == 0, c == 1)
        MLP1 = len(strips)
        mlp_strips(a["w_up"], a["w_down"], 1, 0)
        IN2 = len(strips)
        for c in range(9):
            if c == 5:
                RAW_W1 = len(halves)
                halves.append((a["cmp_k_w1_2"][0].rearrange("(k p) n -> p k n", p=P)[:, 0:8, :], 2048, None))
            col_strip(a["w_in_2"], 512 * c, min(512, GM - 512 * c), "tok", 1)
        for c in range(4):
            col_strip(a["w_in_2"], GM + 512 * c, 512, "tok", 1)
        row_strip([(a["w_o_a_2"], 0), (a["w_o_a_2"], 256)], 0, 0, True, False)
        row_strip([(a["w_o_a_2"], 512), (a["w_o_b_2"], 0)], 0, 4, False, True, "mixed")
        for c in range(2):
            row_strip([(a["w_out_2"], 512 * c), (a["w_out_2"], 512 * c + 256)], 1, 4 * c, c == 0, c == 1)
        MLP2 = len(strips)
        mlp_strips(a["w_up_2"], a["w_down_2"], 0, 1)
        NS = len(strips)
        def pieces(q, size):
            return [(0, size // 2), (size // 2, size)] if q == 0 else [(0, size)]

        def los(n):
            return n + 1 - (n >= 1) - (n >= RAW_W1)

        W1_PARTS = [(kT.rearrange("p (k n) -> p k n", n=256), "cmp_k_w1_2", 8, 6),
                    (gbuf[1][:, 512:1024].rearrange("p (k n) -> p k n", n=256), "cmp_k_w1_2", 14, 2),
                    (u2[:, 0, 2560:4096].rearrange("p (k n) -> p k n", n=256), "cmp_v_w1_2", 0, 6),
                    (u2[:, 1, 2560:4096].rearrange("p (k n) -> p k n", n=256), "cmp_v_w1_2", 6, 6),
                    (AR[:, 16200:16712].rearrange("p (k n) -> p k n", n=256), "cmp_v_w1_2", 12, 2),
                    (xn[:, 1, 512:1024].rearrange("p (k n) -> p k n", n=256), "cmp_v_w1_2", 14, 2)]
        half_of = {}
        for n, (_, _, s) in enumerate(halves):
            if s is not None:
                half_of.setdefault(s, []).append(n)

        W1_AT = (half_of[IN2 + 2][1], half_of[IN2 + 3][0], half_of[IN2 + 3][1])

        evacs, pair_user, turn = 0, {0: 0, 1: 0, 2: 0, 3: 0}, 0
        for s, d in enumerate(strips):
            if d["mode"] in ("tok", "T"):
                d["pair"] = 2 * (turn % 2) if not 6 <= s <= 9 else 2 * (s == 7)
                turn += 1
                banks = [d["pair"], d["pair"] + 1]
            elif d["mode"] == "up":
                continue
            else:
                banks = [0, 1, 2, 3]
            d["need_evac"] = max(pair_user[b] for b in banks)
            if d["mode"] in ("tok", "T") or d["last"]:
                evacs += 1
                d["evac"] = evacs
                for b in banks:
                    pair_user[b] = evacs

        BANKED = [s for s, d in enumerate(strips) if d.get("last")]
        GAIN_OF = {11: 2, 15: 3, IN2 + 16: 6}

        def yb_bank(b):
            return 4 + (TB_Y2 + 4 + b) % 4

        MLP_TURNS = FF // 512 // 2 - 1

        def up_strip(base, j):
            return base + (0 if j == 0 else 2 * j - 1)

        def down_strip(base, j):
            return base + (15 if j == 7 else 2 * j + 2)

        units = []

        for t, hs in [(0, (0, 1)), (0, (2, 3)), (1, (0,)), (1, (1,)), (1, (2,)), (1, (3,))]:
            w = P * (t + 1)
            segs = []
            for hh in hs:
                for c in range(2):
                    r = slice(64 * c, 64 * c + 64)
                    segs.append(dict(
                        row=64 * c, qk=[(qaT[r, 256 * hh + P * t:256 * hh + P * t + P], kaT[r, 256 * hh:256 * hh + w])],
                        mask=[(w - P, maskb(C_CAUS, P))],
                        v=[u_va[:, k, P * hh:P * hh + P] for k in range(t + 1)], vw=P))
            units.append(dict(kind="diff", t=t, hs=hs, w=w, segs=segs, pr=pr1))
        U_X = len(units)
        for t in range(NT):
            for pair in range(2):
                segs = []
                for hh in (2 * pair, 2 * pair + 1):
                    segs.append(dict(
                        row=0, qk=[(qxT[:, 256 * k + P * t:256 * k + P * t + P], kmT[:, 256 * k:256 * k + 256])
                            for k in (2 * hh, 2 * hh + 1)],
                        mask=[], v=[vm[:, k, 256 * hh:256 * hh + 256] for k in range(NT)], vw=256))
                units.append(dict(kind="cross", t=t, hs=(2 * pair, 2 * pair + 1), w=256, segs=segs, pr=pr1))
        U_A = len(units)
        for t in range(NT):
            w = P * (t + 1)
            n = 4 if t == 0 else 2
            for u in range(12 // n):
                hs = tuple(range(n * u, n * u + n))
                segs = []
                for hh in hs:
                    r = slice(64 * (hh % 2), 64 * (hh % 2) + 64)
                    g = hh // 4
                    segs.append(dict(
                        row=r.start, qk=[(qbT[r, 256 * (hh // 2) + P * t:256 * (hh // 2) + P * t + P],
                             kbT[r, 256 * (hh // 2):256 * (hh // 2) + w])],
                        mask=[(0, maskb(C_DIL + 384 * g + P * t, w))],
                        v=[u2[:, k, VB + 64 * hh:VB + 64 * hh + 64] for k in range(t + 1)], vw=64))
                units.append(dict(kind="dil", t=t, hs=hs, w=w, segs=segs, pr=pr2))
        U_N = len(units)
        for t in range(NT):
            w = P * (t + 1)
            for u in range(6 if t == 0 else 12):
                hs = (2 * u, 2 * u + 1) if t == 0 else (u,)
                segs = []
                for hh in hs:
                    r = slice(64 * (hh % 2), 64 * (hh % 2) + 64)
                    g = hh // 4
                    for b, vcol in ((0, VS), (1, VW)):
                        kc = 768 * b + 256 * g
                        segs.append(dict(
                            row=r.start, qk=[(qT[r, 256 * (hh // 2) + P * t:256 * (hh // 2) + P * t + P], kT[r, kc:kc + w])],
                            mask=[(w - P, maskb(C_CAUS, P))],
                            v=[u2[:, k, vcol + 64 * g:vcol + 64 * g + 64] for k in range(t + 1)], vw=64))
                units.append(dict(kind="nsa", t=t, hs=hs, w=w, segs=segs, pr=pr2))
        NU = len(units)
        dil_den, dil_nm = small(24), small(24)

        def den_of(n):
            u = units[n]
            if u["kind"] == "dil":
                b = 12 * u["t"] + u["hs"][0]
                return dil_den[:, b:b + len(u["segs"])], dil_nm[:, b:b + len(u["segs"])]
            return den[:, 4 * n:4 * n + len(u["segs"])], nmx[:, 4 * n:4 * n + len(u["segs"])]

        NORMS = ["g_mix", "g_mem", "g_cross", "g_mlp", "g_final", "norm1_g_2", "norm2_g_2"]

        FILLS = [(0, 0), (1, 0), (0, 6), (1, 10), (0, 12), (1, 14), (1, MLP1 + 14),
                 (0, MLP1 + 16), (1, IN2 + 13), (0, IN2 + 15)]

        def gain_src(g):
            v = a[NORMS[g]]
            v = v if len(v.shape) == 1 else v[0]
            return v.partition_broadcast(P)

        def raw_wait(eng, n):
            eng.wait_ge(raw_loaded[n % 3], 16 * (n // 3 + 1))

        block = ctx.enter_context(nc.Block())

        @block.sync
        def _(sp):
            sp.dma_start(h[:, :, :], a["x"].rearrange("o (t p) d -> p (o t) d", p=P)).then_inc(x_loaded, 16)
            sp.dma_start(gbuf[0][:, :], gain_src(0)).then_inc(gain_loaded[0], 16)
            sp.dma_start(cst[:, :], a["cst"][:, 0:C_SMALL]).then_inc(cst_loaded, 16)
            misc = []
            for n, name in enumerate(("lambda_q1", "lambda_q2", "lambda_k1", "lambda_k2")):
                misc.append((lamv[:, 64 * n:64 * n + 64], a[name][0].partition_broadcast(P)))
            misc.append((gsub, a["g_subln"][0].partition_broadcast(P)))
            for n, name in enumerate(("q_norm_a_2", "k_norm_slc_2", "k_norm_win_2", "q_norm_b_2",
                                      "k_norm_b_2", "k_norm_cmp_2")):
                misc.append((gq[:, 64 * n:64 * n + 64], a[name][0].partition_broadcast(P)))
            for n, name in enumerate(("cmp_k_pos_2", "cmp_v_pos_2")):
                misc.append((vecs[16 * n:16 * n + 16, :], a[name][0].rearrange("(t q) d -> t (q d)", q=2)))
            for n, name in enumerate(("cmp_k_w2_2", "cmp_v_w2_2")):
                misc.append((w2sb[:, n, :, :], a[name][0].rearrange("(k p) n -> p k n", p=P)))
            misc.insert(0, (posi[:, :], a["positions"][0].rearrange("(t p) -> p t", p=P)))
            gains_at = {18: 2, 26: 3, 36: 4, 38: 5, half_of[IN2 + 13][0]: 6}
            for n, (src, size, s) in enumerate(halves):
                if n in W1_AT:
                    sp.wait_ge(norm_used, 4)
                    sp.wait_ge(tb_done, 32)
                    for dst, kv, k0, nk in W1_PARTS[2 * W1_AT.index(n):2 * W1_AT.index(n) + 2]:
                        src1 = a[kv][0].rearrange("(k p) n -> p k n", p=P)[:, k0:k0 + nk, :]
                        sp.dma_start(dst, src1).then_inc(w1_loaded, 16)
                if n in gains_at:
                    g = gains_at[n]
                    sp.wait_ge(norm_used, g - 1)
                    if g == 6:
                        sp.wait_ge(gates_in, 2)
                    sp.dma_start(gbuf[g % 2][:, :], gain_src(g)).then_inc(gain_loaded[g], 16)
                if n >= 3:
                    if n - 3 < 2:
                        sp.wait_ge(lo_first, n - 2)
                    if n - 3 == 0:
                        sp.wait_ge(lo_done, 1)
                    elif n - 3 == 1:
                        pass
                    elif n - 3 == RAW_W1:
                        sp.wait_ge(raw_used, 1)
                    else:
                        sp.wait_ge(lo_done, los(n - 3))
                dst = RAW[n % 3][:, 0:size].rearrange("p (k n) -> p k n", k=src.shape[1])
                sp.dma_start(dst, src).then_inc(raw_loaded[n % 3], 16)
                if n == 3:
                    sp.dma_start(memx, a["mem"].rearrange("o (t p) d -> p (o t) d", p=P)).then_inc(mem_loaded, 16)
                    sp.dma_start(gbuf[1][:, :], gain_src(1)).then_inc(gain_loaded[1], 16)
                if n == 4:
                    sp.dma_start(AR[:, 0:C_ALL - C_SMALL], a["cst"][:, C_SMALL:C_ALL]).then_inc(msk_loaded, 16)
                with nc.allow_non_contiguous_dma(reason="one position per partition"):
                    for small_dst, small_src in misc[6 * (n - 5):6 * (n - 4)] if 5 <= n <= 7 else []:
                        sp.dma_start(small_dst, small_src).then_inc(misc_loaded, 16)
            for b in range(4):
                t, c = b // 2, slice(512 * (b % 2), 512 * (b % 2) + 512)
                sp.wait_ge(res_done, b + 1)
                sp.dma_start(out[0, P * t:P * t + P, c], h[:, t, c]).then_inc(out_stored, 16)
            sp.wait_ge(out_stored, 64)

        @block.gpsimd
        def _(pool):
            for s in range(NS):
                if s == IN2 + 13:
                    pool.wait_ge(dl_weights, 1)
                    for t in range(NT):
                        o = u2[:, t, 512:1280].rearrange("p (s c) -> p s c", c=64)
                        G = nc.gpsimd
                        G.tensor_tensor(o, o, dl[1][:, 12 * t:12 * t + 12].unsqueeze(2).broadcast_to([P, 12, 64]),
                                        ALU.mult).then_inc(pool_step, 1)
                        pool.wait_ge(pool_step, 2 * t + 1)
                        G.tensor_tensor(u2[:, t, 512:768], u2[:, t, 512:768], u2[:, t, 768:1024],
                                        ALU.add).then_inc(pool_step, 1)
                        pool.wait_ge(pool_step, 2 * t + 2)
                        G.tensor_tensor(xn[:, t, 768:1024], u2[:, t, 512:768], u2[:, t, 1024:1280],
                                        ALU.add).then_inc(dl_mixed, 1)
                for q, n in enumerate(half_of[s]):
                    if s == 0 and q == 1:
                        continue
                    parts = pieces(q, halves[n][1])[:1 if s == 0 else 2]
                    for i, (c0, c1) in enumerate(parts):
                        pool.wait_ge(hi_done, 3 * s + 2 * q + i + 1)
                        x = nc.gpsimd.tensor_tensor(LO[s % 2][:, 2048 * q + c0:2048 * q + c1], RAW[n % 3][:, c0:c1],
                                                    HI[s % 2][:, 2048 * q + c0:2048 * q + c1].bitcast(f32),
                                                    ALU.subtract)
                        if i == len(parts) - 1:
                            x.then_inc(lo_done, 1)

        @block.scalar
        def _(act):
            chain = [0]

            def link(ins):
                chain[0] += 1
                ins.then_inc(act_step, 1)
                act.wait_ge(act_step, chain[0])

            def norm_stats(i, src):
                if i == 1:
                    act.wait_ge(norm_used, i)
                junk = AR[:, 4096:5120] if i == 0 else sq_junk
                for t in range(NT):
                    link(nc.scalar.activation(xn[:, t, :] if i == 1 else junk, src[:, t, :], ACT.Square,
                                              accum_out=ss_n[:, 2 * i + t:2 * i + t + 1]))
                c = slice(2 * i, 2 * i + 2)
                link(nc.scalar.activation(nr_n[:, c], ss_n[:, c], ACT.Ln, scale=1.0 / D, bias=eps))
                nc.scalar.activation(y0_n[:, c], nr_n[:, c], ACT.Exp, scale=-0.5).then_inc(norm_sq, 1)

            strip_n = [0]

            def hi(s, part=None):
                assert s == strip_n[0]
                strip_n[0] += part != 0
                if s >= 2 and part != 1:
                    act.wait_ge(strip_done, s - 1)
                for q, n in enumerate(half_of[s]):
                    if part is not None and q != part:
                        continue
                    raw_wait(act, n)
                    for c0, c1 in pieces(q, halves[n][1]):
                        nc.scalar.activation(HI[s % 2][:, 2048 * q + c0:2048 * q + c1], RAW[n % 3][:, c0:c1],
                                             ACT.Copy).then_inc(hi_done, 1)

            tb = [0]
            fill = [0]

            def fill_hi():
                buf, done = FILLS[fill[0]]
                act.wait_ge(strip_done, done)
                for b in range(4):
                    t, kh = b // 2, b % 2
                    act.wait_ge(tb_done, tb[0] + 1)
                    dst = XH[buf][:, 1024 * kh:1024 * kh + 1024].rearrange("p (k u) -> p k u", u=S)
                    src = bank(4 + tb[0] % 4).rearrange("p (k u) -> p k u", u=P)
                    nc.scalar.activation(dst[:, :, P * t:P * t + P], src, ACT.Copy).then_inc(tb_hi, 1)
                    tb[0] += 1
                fill[0] += 1

            def exps(n):
                u = units[n]
                dn, nm = den_of(n)
                act.wait_ge(mx_done, n + 1)
                if n >= 2:
                    act.wait_ge(tr_done, n - 1)
                last = len(u["segs"]) - 1
                for i in range(last + 1):
                    c = slice(u["w"] * i, u["w"] * i + u["w"])
                    x = nc.scalar.activation(u["pr"][n % 2][:, c], bank(4 + n % 2)[:, c], ACT.Exp,
                                             bias=nm[:, i:i + 1], accum_out=dn[:, i:i + 1])
                    if i == last:
                        x.then_inc(ex_done, 1)

            act.wait_ge(rope_arg, 1)
            nc.scalar.activation(lame[:, 0:1], eps, ACT.Copy)
            fill_hi()
            hi(0)
            hi(1)
            act.wait_ge(x_loaded, 16)
            act.wait_ge(rope_arg, 1)
            norm_stats(0, h)
            hi(2)
            act.wait_ge(mem_loaded, 16)
            act.wait_ge(tb_done, 4)
            norm_stats(1, memx)
            hi(3)
            act.wait_ge(rope_arg, 2)
            nc.scalar.activation(scs, ang, ACT.Sin).then_inc(rope_sin, 1)
            act.wait_ge(lam_arg, 1)
            nc.scalar.activation(lame, lams, ACT.Exp).then_inc(lam_exp, 1)
            hi(4)
            fill_hi()
            tb[0] += 4
            hi(5)
            hi(6)
            hi(7)
            for n in range(U_X):
                exps(n)
                if n >= 4:
                    hi(8, n - 4)
            for half in range(2):
                if half == 0:
                    hi(9, 0)
                js = (2 * half, 2 * half + 1)
                for j in js:
                    act.wait_ge(z_done, j + 1)
                    if j >= 2:
                        act.wait_ge(z_cum, j - 1)
                    link(nc.scalar.activation(sbz[j % 2], bank(4 + 2 * (j % 2), 2)[:, 0:768], ACT.Abs))
                for j in js:
                    link(nc.scalar.activation(sbz[j % 2], sbz[j % 2], ACT.Exp, scale=-1.0))
                for j in js:
                    nc.scalar.activation(sbz[j % 2], sbz[j % 2], ACT.Ln, bias=1.0).then_inc(z_ln, 1)
                if half == 0:
                    act.wait_ge(sub_sq, 1)
                    link(nc.scalar.activation(y0_s, ss_s, ACT.Ln, scale=1.0 / P, bias=eps))
                    nc.scalar.activation(y0_s, y0_s, ACT.Exp, scale=-0.5).then_inc(sub_y0, 1)
                    hi(9, 1)
                for j in (2 * half, 2 * half + 1):
                    act.wait_ge(z_cum, j + 1)
                    if j >= 2:
                        act.wait_ge(z_pv, j - 1)
                    nc.scalar.activation(sba[j % 2], bank(4 + 2 * (j % 2), 2)[:, 0:768], ACT.Exp).then_inc(z_at, 1)
                hi(10 + half)
            fill_hi()
            hi(12)
            fill_hi()
            hi(13)
            act.wait_ge(src_ready, 1)
            norm_stats(2, h)
            hi(14)
            hi(15)
            for n in range(U_X, U_A):
                exps(n)
            fill_hi()
            hi(16)
            fill_hi()
            hi(17)
            act.wait_ge(src_ready, 2)
            norm_stats(3, h)

            def mlp(base, a0, abuf, before):
                for i in range(2, 16):
                    hi(base + i)
                    for j in range(8):
                        if up_strip(0, j) == i - 2:
                            act.wait_ge(sq_ready, a0 + j + 1)
                            act.wait_ge(strip_done, down_strip(base, j - 2) + 1 if j >= 2 else before)
                            c = slice(1024 * (j % 2), 1024 * (j % 2) + 1024)
                            nc.scalar.activation(XH[abuf][:, c], act_q, ACT.Copy).then_inc(a_hi, 1)

            mlp(MLP1, 0, 0, MLP1)
            hi(IN2)
            fill_hi()
            hi(IN2 + 1)
            act.wait_ge(src_ready, 3)
            norm_stats(4, h)
            hi(IN2 + 2)
            act.wait_ge(src_ready, 4)
            norm_stats(5, h)

            def head_stats(i, col, heads):
                v = sqb[:, 0:128 * heads].rearrange("p (t c) -> p t c", t=NT)
                if i:
                    act.wait_ge(hn_done, i)
                nc.scalar.activation(v, u2[:, :, col:col + 64 * heads], ACT.Square).then_inc(hn_sq, 1)
                act.wait_ge(hn_ss, i + 1)
                m = 2 * heads
                link(nc.scalar.activation(y0_h[:, 0:m], ss_h[:, 0:m], ACT.Ln, scale=1.0 / HD, bias=eps))
                nc.scalar.activation(y0_h[:, 0:m], y0_h[:, 0:m], ACT.Exp, scale=-0.5).then_inc(hn_y0, 1)

            hi(IN2 + 3)
            act.wait_ge(evac_done, strips[IN2 + 1]["evac"])
            head_stats(0, QA, 12)
            hi(IN2 + 4)
            hi(IN2 + 5)
            act.wait_ge(evac_done, strips[IN2 + 3]["evac"])
            head_stats(1, KS, 3)
            head_stats(2, KW, 3)
            hi(IN2 + 6)
            act.wait_ge(sg_arg, 1)
            nc.scalar.activation(sgn, sgn, ACT.Exp, scale=-1.0).then_inc(sg_exp, 1)
            act.wait_ge(ge_arg, 1)
            nc.scalar.activation(hu, hu, ACT.Exp).then_inc(ge_exp, 1)
            hi(IN2 + 7)
            act.wait_ge(kc_ss, 1)
            link(nc.scalar.activation(y0_h[0:15, 0:3], ss_h[0:15, 0:3], ACT.Ln, scale=1.0 / HD, bias=eps[0:15, :]))
            nc.scalar.activation(y0_h[0:15, 0:3], y0_h[0:15, 0:3], ACT.Exp, scale=-0.5).then_inc(kc_y0, 1)
            act.wait_ge(evac_done, strips[IN2 + 5]["evac"])
            head_stats(3, QB, 12)
            hi(IN2 + 8)
            act.wait_ge(evac_done, strips[IN2 + 6]["evac"])
            head_stats(4, KB, 12)
            hi(IN2 + 9)
            act.wait_ge(cs_arg, 1)
            nc.scalar.activation(scb[:, :], scb[:, :], ACT.Exp).then_inc(cs_exp, 1)
            hi(IN2 + 10)
            hi(IN2 + 11)
            for n in range(U_A, NU):
                exps(n)
                if n - U_A in (1, 2):
                    hi(IN2 + 12, n - U_A - 1)
                if n - U_A in (14, 15):
                    hi(IN2 + 13, n - U_A - 14)
                if n == U_N + 2:
                    act.wait_ge(dl_den, 1)
                    nc.scalar.activation(dl[0], dil_den, ACT.Ln).then_inc(dl_ln, 1)
                if n == U_N + 4:
                    act.wait_ge(dl_arg, 1)
                    nc.scalar.activation(dl[1], dl[1], ACT.Exp).then_inc(dl_exp, 1)
            tb[0] = TB_Y2
            fill_hi()
            hi(IN2 + 14)
            act.wait_ge(gates_in, 4)
            for c, w in ((QB, 1536), (QA, 512)):
                nc.scalar.activation(u2[:, :, c:c + w], u2[:, :, c:c + w], ACT.Sigmoid).then_inc(gates_sig, 1)
            hi(IN2 + 15)
            fill_hi()
            hi(IN2 + 16)
            hi(MLP2)
            fill_hi()
            hi(MLP2 + 1)
            act.wait_ge(src_ready, 5)
            norm_stats(6, h)
            mlp(MLP2, 8, 1, MLP2)

        @block.vector
        def _(dve):
            chain = [0]
            V = nc.vector
            marked = [0]
            bcasts = [0]

            def link(ins):
                chain[0] += 1
                ins.then_inc(dve_step, 1)
                dve.wait_ge(dve_step, chain[0])

            def signal(sm, n):
                cell = marks[:, marked[0]:marked[0] + 1]
                marked[0] += 1
                assert marked[0] <= marks.shape[1]
                V.tensor_copy(cell, eps).then_inc(sm, n)

            def newton(r, ss, y0, width):
                n = ss.shape[1]
                p = ss.shape[0]
                m, q = t_nr1[0:p, 0:n], t_nr2[0:p, 0:n]
                link(V.tensor_scalar(m, ss, 1.0 / width, EPS, ALU.mult, ALU.add))
                link(V.tensor_tensor(q, y0, y0, ALU.mult))
                link(V.tensor_tensor(q, q, m, ALU.mult))
                link(V.tensor_scalar(q, q, -0.5, 1.5, ALU.mult, ALU.add))
                link(V.tensor_tensor(r, y0, q, ALU.mult))

            def bc(ap, shape):
                return ap.broadcast_to(shape)

            tb = [0]
            fill = [0]

            def norm_apply(i, src, dst, into_xn):
                dve.wait_ge(norm_sq, i + 1)
                dve.wait_ge(gain_loaded[i], 16)
                newton(rstd_n[:, 2 * i:2 * i + 2], ss_n[:, 2 * i:2 * i + 2], y0_n[:, 2 * i:2 * i + 2], D)
                for t in range(NT):
                    x = V.scalar_tensor_tensor(dst[:, t, :], src[:, t, :], rstd_n[:, 2 * i + t:2 * i + t + 1],
                                               gbuf[i % 2][:, :], ALU.mult, ALU.mult)
                    if into_xn:
                        x.then_inc(xn_ready, 2)
                    else:
                        link(x)
                signal(norm_used, 1)

            def fill_lo():
                buf, done = FILLS[fill[0]]
                dve.wait_ge(strip_done, done)
                for b in range(4):
                    t, kh = b // 2, b % 2
                    dve.wait_ge(tb_hi, 4 * fill[0] + b + 1)
                    c = slice(1024 * kh, 1024 * kh + 1024)
                    dst = XL[buf][:, c].rearrange("p (k u) -> p k u", u=S)[:, :, P * t:P * t + P]
                    sub = XH[buf][:, c].bitcast(f32).rearrange("p (k u) -> p k u", u=S)[:, :, P * t:P * t + P]
                    src = bank(4 + tb[0] % 4).rearrange("p (k u) -> p k u", u=P)
                    V.tensor_tensor(dst, src, sub, ALU.subtract).then_inc(tb_evac, 1)
                    tb[0] += 1
                fill[0] += 1

            def tb_take(fn, last=None):
                dve.wait_ge(tb_done, tb[0] + 1)
                fn(bank(4 + tb[0] % 4)).then_inc(tb_evac, 1)
                tb[0] += 1
                dve.wait_ge(tb_evac, tb[0])

            def evac(s, dst, scale=None, rows=None, rb=False):
                d = strips[s]
                dve.wait_ge(strip_done, s + 1)
                src = bank(d["pair"], 2)
                if d["mode"] == "tok":
                    src = src.rearrange("p (t c) -> p t c", t=NT)[:, :, 0:d["w"]]
                if rows is not None:
                    V.tensor_tensor(dst, src, bc(rows.unsqueeze(2), [P, NT, d["w"]]), ALU.mult).then_inc(evac_done, 1)
                elif rb:
                    V.scalar_tensor_tensor(dst.rearrange("p (c u) -> p c u", u=S),
                                           src.rearrange("p (c u) -> p c u", u=S), scale,
                                           bc(rB.unsqueeze(1), [P, 4, S]), ALU.mult, ALU.mult).then_inc(evac_done, 1)
                elif scale is None:
                    V.tensor_copy(dst, src).then_inc(evac_done, 1)
                else:
                    V.tensor_scalar(dst, src, scale, None, ALU.mult).then_inc(evac_done, 1)
                dve.wait_ge(evac_done, d["evac"])

            def bank_wait(r, b):
                if b < 3:
                    dve.wait_ge(bank_done, 3 * r + b + 1)
                else:
                    dve.wait_ge(strip_done, BANKED[r] + 1)

            def residual(s, gain):
                r = BANKED.index(s)
                for b in range(4):
                    t, c = b // 2, slice(512 * (b % 2), 512 * (b % 2) + 512)
                    bank_wait(r, b)
                    x = V.tensor_tensor(h[:, t, c], h[:, t, c], bank(b), ALU.add)
                    if gain is None:
                        x.then_inc(res_done, 1)
                        continue
                    link(x)
                    if b == 0 and s in GAIN_OF:
                        dve.wait_ge(gain_loaded[GAIN_OF[s]], 16)
                    V.tensor_tensor(xn[:, t, c], h[:, t, c], gain[:, c], ALU.mult).then_inc(xn_ready, 1)
                if gain is not None:
                    signal(evac_done, 1)
                    signal(src_ready, 1)

            def row_scale(i):
                dve.wait_ge(norm_sq, i + 1)
                newton(rstd_n[:, 2 * i:2 * i + 2], ss_n[:, 2 * i:2 * i + 2], y0_n[:, 2 * i:2 * i + 2], D)

            def broadcast_rstd(i, dst):
                for t in range(NT):
                    x = V.tensor_scalar(diag[:, P * t:P * t + P], ident, rstd_n[:, 2 * i + t:2 * i + t + 1], None,
                                        ALU.mult)
                    x.then_inc(diag_ready, 1)
                bcasts[0] += 1
                dve.wait_ge(rb_done, bcasts[0])
                V.tensor_scalar(rB, dst[:, 0:S], -1.0, None, ALU.mult).then_inc(rb_taken, 1)
                dve.wait_ge(rb_taken, bcasts[0])

            V.memset(eps, EPS).then_inc(rope_arg, 1)
            dve.wait_ge(rope_arg, 1)
            dve.wait_ge(x_loaded, 16)
            dve.wait_ge(gain_loaded[0], 16)
            for b in range(4):
                t, c = b // 2, slice(512 * (b % 2), 512 * (b % 2) + 512)
                V.tensor_tensor(xn[:, t, c], h[:, t, c], gbuf[0][:, c], ALU.mult).then_inc(xn_ready, 1)
            signal(norm_used, 1)
            fill_lo()
            for n_hi, raw, c0, c1 in ((2, 0, 1024, 2048), (3, 1, 2048, 4096)):
                dve.wait_ge(hi_done, n_hi)
                V.tensor_tensor(LO[0][:, c0:c1], RAW[raw][:, c0 - 2048 * raw:c1 - 2048 * raw],
                                HI[0][:, c0:c1].bitcast(f32), ALU.subtract).then_inc(lo_first, 1)
            dve.wait_ge(msk_loaded, 16)
            V.tensor_copy(mbf[:, P:], AR[:, 0:C_ALL - C_SMALL]).then_inc(masks_ready, 1)
            V.tensor_copy(identb, ident).then_inc(masks_ready, 1)
            dve.wait_ge(masks_ready, 2)
            row_scale(0)
            evac(0, u_qa, rows=rstd_n[:, 0:2])
            norm_apply(1, memx, xn, True)
            dve.wait_ge(cst_loaded, 16)
            dve.wait_ge(misc_loaded, 16 * 16)
            link(V.tensor_copy(posf, posi[:, :]))
            inv = cst[:, C_INV:C_INV + 8]
            base = rp[:, 0:32].rearrange("p (s t f) -> p s t f", s=2, t=NT)
            for sc in range(2):
                link(V.tensor_tensor(base[:, sc], bc(posf.unsqueeze(2), [P, NT, 8]),
                                     bc(inv.unsqueeze(1), [P, NT, 8]), ALU.mult))
                link(V.tensor_scalar(rn[:, 16 * sc:16 * sc + 16], rp[:, 16 * sc:16 * sc + 16],
                                     1.0 / (2 * math.pi), 0.25 * sc, ALU.mult, ALU.add))
            link(V.tensor_scalar(rn, rn, BIG, -BIG, ALU.add, ALU.add))
            cur = rp[:, 0:32]
            for piece in TWO_PI:
                link(V.scalar_tensor_tensor(ang, rn, -piece, cur, ALU.mult, ALU.add))
                cur = ang
            link(V.tensor_scalar(ang[:, 16:32], ang[:, 16:32], math.pi / 2, None, ALU.add))
            V.tensor_scalar(ang, ang, PI_LOW, -PI_LOW, ALU.min, ALU.max).then_inc(rope_arg, 1)
            link(V.tensor_tensor(lamp, lamv[:, 0:128], lamv[:, 128:256], ALU.mult))
            V.tensor_reduce(lams, lamp.rearrange("p (a c) -> p a c", a=2), AX.X, ALU.add).then_inc(lam_arg, 1)

            def rope1(u):
                v = u.rearrange("p t (m c) -> p t m c", c=HD)
                x1, x2 = v[:, :, :, 0:8], v[:, :, :, 8:16]
                tmp = [rp[:, 128 * i:128 * i + 128].rearrange("p (t m f) -> p t m f", t=NT, m=8) for i in range(4)]
                sc = scs.rearrange("p (s t f) -> p s t f", s=2, t=NT)
                sn = bc(sc[:, 0].unsqueeze(2), [P, NT, 8, 8])
                cs = bc(sc[:, 1].unsqueeze(2), [P, NT, 8, 8])
                link(V.tensor_tensor(tmp[0], x1, cs, ALU.mult))
                link(V.tensor_tensor(tmp[1], x2, sn, ALU.mult))
                link(V.tensor_tensor(tmp[2], x2, cs, ALU.mult))
                link(V.tensor_tensor(tmp[3], x1, sn, ALU.mult))
                link(V.tensor_tensor(x1, tmp[0], tmp[1], ALU.subtract))
                V.tensor_tensor(x2, tmp[2], tmp[3], ALU.add).then_inc(qk_ready, 1)

            evac(1, u_ka, rows=rstd_n[:, 0:2])
            dve.wait_ge(rope_sin, 1)
            rope1(u_qa)
            dve.wait_ge(qk_ready, 1)
            rope1(u_ka)
            evac(2, u_va, rows=rstd_n[:, 0:2])
            broadcast_rstd(0, bank(4))
            evac(3, qsT, 0.125, rb=True)
            fill_lo()
            for x, dst, scale in ((0, qaT, 0.125), (1, kaT, 1.0)):
                for b in range(2):
                    tb_take(lambda src: V.tensor_scalar(dst[:, 512 * b:512 * b + 512], src, scale, None, ALU.mult))
            evac(4, ksT, 1.0, rb=True)
            evac(5, u_vs, rows=rstd_n[:, 0:2])

            def unit_loop(n0, n1, post, hook):
                for i in range(n0, n1 + 2):
                    if i < n1:
                        u = units[i]
                        dve.wait_ge(sc_done, i + 1)
                        src = bank(4 + i % 2).rearrange("p (s w) -> p s w", w=u["w"])
                        V.tensor_reduce(den_of(i)[1], src, AX.X, ALU.max, negate=True).then_inc(mx_done, 1)
                    if n0 <= i - 1 < n1:
                        dve.wait_ge(tr_done, i)
                        if i - 1 >= 2:
                            dve.wait_ge(pv_done, i - 2)
                        V.tensor_copy(units[i - 1]["pr"][2 + (i - 1) % 2], bank(6)).then_inc(pt_done, 1)
                    if i - 2 >= n0:
                        dve.wait_ge(pv_done, i - 1)
                        post(i - 2, units[i - 2])
                    hook(i)

            def post_diff(n, u):
                k = len(u["segs"])
                nh = k // 2
                link(V.reciprocal(coef[:, 0:k], den_of(n)[0]))
                cv = coef[:, 0:k].rearrange("p (h c) -> p h c", c=2)
                link(V.tensor_scalar(cv[:, :, 1], cv[:, :, 1], nlam, None, ALU.mult))
                o = bank(7)[:, 0:P * k].rearrange("p (s c) -> p s c", c=P)
                w = comb1[:, 0:P * k]
                V.tensor_tensor(w.rearrange("p (s c) -> p s c", c=P), o,
                                bc(coef[:, 0:k].unsqueeze(2), [P, k, P]), ALU.mult).then_inc(post_done, 1)
                dve.wait_ge(post_done, n + 1)
                wv = w.rearrange("p (h c d) -> p h c d", c=2, d=P)
                y = xn[:, u["t"], P * u["hs"][0]:P * u["hs"][0] + P * nh].rearrange("p (h d) -> p h d", d=P)
                link(V.tensor_tensor(y, wv[:, :, 0, :], wv[:, :, 1, :], ALU.add))

            def hook_diff(i):
                if i == 4:
                    evac(6, kmT[:, 0:1024])
                if i == 7:
                    evac(7, kmT[:, 1024:2048])

            dve.wait_ge(tb_done, 8)
            link(V.tensor_scalar(gsub, gsub, 1.0 - LAM_INIT, None, ALU.mult))
            dve.wait_ge(lam_exp, 1)
            link(V.tensor_tensor(nlam, lame[:, 1:2], lame[:, 0:1], ALU.subtract))
            link(V.tensor_scalar(nlam, nlam, -LAM_INIT, None, ALU.add))
            unit_loop(0, U_X, post_diff, hook_diff)
            def sub_norm():
                ya = xn[:, :, 0:512]
                link(V.tensor_tensor(sq1.rearrange("p (t c) -> p t c", t=NT), ya, ya, ALU.mult))
                V.tensor_reduce(ss_s, sq1.rearrange("p (s c) -> p s c", c=P), AX.X, ALU.add).then_inc(sub_sq, 1)
                dve.wait_ge(sub_y0, 1)
                newton(rs_s, ss_s, y0_s, P)
                yv = ya.rearrange("p t (h c) -> p t h c", c=P)
                rv = rs_s.rearrange("p (t h) -> p t h", t=NT)
                link(V.tensor_tensor(yv, yv, bc(rv.unsqueeze(3), [P, NT, 4, P]), ALU.mult))
                link(V.tensor_tensor(yv, yv, bc(gsub.unsqueeze(1).unsqueeze(1), [P, NT, 4, P]), ALU.mult))

            for half in range(2):
                for j in (2 * half, 2 * half + 1):
                    dve.wait_ge(z_ln, j + 1)
                    V.scalar_tensor_tensor(sbz[j % 2], bank(4 + 2 * (j % 2), 2)[:, 0:768], 0.0, sbz[j % 2],
                                           ALU.max, ALU.add).then_inc(z_sp, 1)
                if half == 0:
                    sub_norm()
                evac(8 + half, vm[:, :, 512 * half:512 * half + 512])
            dve.wait_ge(z_pv, 4)
            for t in range(NT):
                V.tensor_copy(xn[:, t, 512:1024], bank(2 + t)).then_inc(xn_ready, 2)
            fill_lo()
            residual(11, gbuf[0])
            signal(norm_used, 1)
            fill_lo()
            row_scale(2)
            broadcast_rstd(2, bank(7))
            evac(12, qxT[:, 0:1024], 0.0625, rb=True)
            evac(13, qxT[:, 1024:2048], 0.0625, rb=True)

            def post_cross(n, u):
                k = 2
                link(V.reciprocal(coef[:, 0:k], den_of(n)[0]))
                o = bank(7).rearrange("p (s c) -> p s c", c=256)
                y = xn[:, u["t"], 256 * u["hs"][0]:256 * u["hs"][0] + 512].rearrange("p (s c) -> p s c", c=256)
                V.tensor_tensor(y, o, bc(coef[:, 0:k].unsqueeze(2), [P, k, 256]), ALU.mult).then_inc(post_done, 1)
                dve.wait_ge(post_done, n + 1)
                signal(xn_ready, 1)

            unit_loop(U_X, U_A, post_cross, lambda i: None)
            fill_lo()
            residual(15, gbuf[1])
            signal(norm_used, 1)
            fill_lo()
            row_scale(3)
            broadcast_rstd(3, bank(0))

            def activate(j, done, a0, abuf, i=None):
                def at(count, per_turn):
                    return count if i is None else i * per_turn + count

                dve.wait_ge(strip_done, at(done, 4))
                V.scalar_tensor_tensor(act_q.rearrange("p (c u) -> p c u", u=S),
                                       bank(4 + 2 * (j % 2), 2).rearrange("p (c u) -> p c u", u=S), 0.0,
                                       bc(rB.unsqueeze(1), [P, 4, S]), ALU.max, ALU.mult).then_inc(up_evac, 1)
                n = a0 + j + 1
                dve.wait_ge(up_evac, at(n, 2))
                V.tensor_tensor(act_q, act_q, act_q, ALU.mult).then_inc(sq_ready, 1)
                dve.wait_ge(sq_ready, at(n, 2))
                dve.wait_ge(a_hi, at(n, 2))
                c = slice(1024 * (j % 2), 1024 * (j % 2) + 1024)
                V.tensor_tensor(XL[abuf][:, c], act_q, XH[abuf][:, c].bitcast(f32), ALU.subtract).then_inc(a_lo, 1)
                dve.wait_ge(a_lo, at(n, 2))

            def mlp(base, a0, abuf):
                for j in (0, 1):
                    activate(j, up_strip(base, j) + 1, a0, abuf)
                if base == MLP1:
                    dve.wait_ge(gain_loaded[4], 16)
                    dve.wait_ge(gain_loaded[5], 16)
                    link(V.tensor_tensor(g45, gbuf[0][:, :], gbuf[1][:, :], ALU.mult))
                with dve.Fori(0, MLP_TURNS) as i:
                    for j in (2, 3):
                        activate(j, up_strip(base, j) + 1, a0, abuf, i)

            mlp(MLP1, 0, 0)
            residual(IN2 - 1, g45)
            fill_lo()
            row_scale(4)
            for t in range(NT):
                link(V.scalar_tensor_tensor(h[:, t, :], h[:, t, :], rstd_n[:, 8 + t:9 + t], gbuf[0][:, :],
                                            ALU.mult, ALU.mult))
            signal(src_ready, 1)
            signal(norm_used, 2)
            row_scale(5)
            link(V.tensor_tensor(r45, rstd_n[:, 8:10], rstd_n[:, 10:12], ALU.mult))

            cs2 = cst[:, C_CS2:C_CS2 + 64].rearrange("p (t f) -> p t f", t=NT)
            sn2 = cst[:, C_SN2:C_SN2 + 64].rearrange("p (t f) -> p t f", t=NT)

            def head_norm(i, col, heads, gain, outs):
                g = gq[:, 64 * gain:64 * gain + 64]
                t1 = T1.rearrange("p (t h f) -> p t h f", t=NT, h=2)
                t2 = T2.rearrange("p (t h f) -> p t h f", t=NT, h=2)
                link(V.tensor_tensor(t1, bc(cs2.unsqueeze(2), [P, NT, 2, 32]),
                                     bc(g.rearrange("p (h f) -> p h f", h=2).unsqueeze(1), [P, NT, 2, 32]), ALU.mult))
                link(V.scalar_tensor_tensor(t2[:, :, 0], sn2, -1.0, bc(g[:, 32:64].unsqueeze(1), [P, NT, 32]),
                                            ALU.mult, ALU.mult))
                link(V.tensor_tensor(t2[:, :, 1], sn2, bc(g[:, 0:32].unsqueeze(1), [P, NT, 32]), ALU.mult))
                x = u2[:, :, col:col + 64 * heads].rearrange("p t (m c) -> p t m c", c=HD)
                n = 128 * heads
                va = ta[:, 0:n].rearrange("p (t m c) -> p t m c", t=NT, c=HD)
                vb = sqb[:, 0:n].rearrange("p (t m c) -> p t m c", t=NT, c=HD)
                link(V.tensor_tensor(va, x, bc(T1.rearrange("p (t c) -> p t c", t=NT).unsqueeze(2),
                                               [P, NT, heads, HD]), ALU.mult))
                dve.wait_ge(hn_sq, i + 1)
                V.tensor_reduce(ss_h[:, 0:2 * heads], sqb[:, 0:n].rearrange("p (s c) -> p s c", c=HD),
                                AX.X, ALU.add).then_inc(hn_ss, 1)
                dve.wait_ge(hn_ss, i + 1)
                t2c = T2.rearrange("p (t c) -> p t c", t=NT)
                for z in range(2):
                    link(V.tensor_tensor(vb[:, :, :, 32 * z:32 * z + 32], x[:, :, :, 32 - 32 * z:64 - 32 * z],
                                         bc(t2c[:, :, 32 * z:32 * z + 32].unsqueeze(2), [P, NT, heads, 32]), ALU.mult))
                link(V.tensor_tensor(va, va, vb, ALU.add))
                dve.wait_ge(hn_y0, i + 1)
                newton(rs_h[:, 0:2 * heads], ss_h[:, 0:2 * heads], y0_h[:, 0:2 * heads], HD)
                r = bc(rs_h[:, 0:2 * heads].rearrange("p (t m) -> p t m", t=NT).unsqueeze(3), [P, NT, heads, HD])
                for o in outs:
                    link(V.tensor_tensor(o, va, r, ALU.mult))
                signal(hn_done, 1)

            def u2_evac(c):
                evac(IN2 + c, u2[:, :, 512 * c:512 * c + strips[IN2 + c]["w"]], rows=r45)

            def dup_views(buf):
                v = buf.rearrange("p (t g d c) -> p t g d c", t=NT, g=3, d=2)
                return [v[:, :, :, 0, :], v[:, :, :, 1, :]]

            u2_evac(0)
            u2_evac(1)
            x = u2[:, :, QA:QA + 768].rearrange("p t (m c) -> p t m c", c=HD)
            head_norm(0, QA, 12, 0, [x])
            u2_evac(2)
            for kv, col in ((0, KC), (1, VC)):
                for o in dup_views(cdup[:, 768 * kv:768 * kv + 768]):
                    link(V.tensor_copy(o, u2[:, :, col:col + 192].rearrange("p t (g c) -> p t g c", g=3)))
            signal(at_ready, 1)
            u2_evac(3)
            gv = sgn.rearrange("p (t c) -> p t c", t=NT)
            V.tensor_scalar(gv, u2[:, :, GA:GA + 36], -80.0, None, ALU.max).then_inc(sg_arg, 1)
            tb_take(lambda src: V.tensor_copy(pe2, src[:, 0:32]))
            for b in range(3):
                dve.wait_ge(tb_done, tb[0] + 1)
                src = bank(4 + tb[0] % 4)
                link(V.tensor_copy(kc2[0:64, 512 * b:512 * b + 512], src[0:64, :]))
                V.tensor_copy(kc2[64:128, 512 * b:512 * b + 512].rearrange("p (g u) -> p g u", u=S)[:, :, 0:S - 1],
                              src[64:128, :].rearrange("p (g u) -> p g u", u=S)[:, :, 1:S]).then_inc(tb_evac, 1)
                tb[0] += 1
                dve.wait_ge(tb_evac, tb[0])
            for kv in range(2):
                at = AT[:, 720 * kv:720 * kv + 720].rearrange("p (y g c) -> p y g c", y=16, g=3)
                src = kc2[:, 768 * kv:768 * kv + 768].rearrange("p (g c y z) -> p y g c z", g=3, y=8, z=2)
                for th in range(2):
                    pe = pe2[:, 16 * kv + 8 * th:16 * kv + 8 * th + 8]
                    link(V.tensor_tensor(at[:, 8 * th:8 * th + 8], src[:, :, :, th:th + CMP_N, 0],
                                         bc(pe.unsqueeze(2).unsqueeze(2), [P, 8, 3, CMP_N]), ALU.add))
            signal(at_ready, 1)
            for b in range(3):
                tb_take(lambda src: V.tensor_scalar(qT[:, 512 * b:512 * b + 512], src, 0.125, None, ALU.mult))
            head_norm(1, KS, 3, 1, dup_views(kdup[0]))
            head_norm(2, KW, 3, 2, dup_views(kdup[1]))
            u2_evac(4)
            tb_take(lambda src: V.tensor_copy(hx, src[:, 0:180]))
            link(V.tensor_tensor(hg, hx, hx, ALU.mult))
            link(V.tensor_scalar(hg, hg, 0.044715, 1.0, ALU.mult, ALU.add))
            link(V.tensor_tensor(hg, hg, hx, ALU.mult))
            V.tensor_scalar(hu, hg, -2.0 * math.sqrt(2.0 / math.pi), 80.0, ALU.mult, ALU.min).then_inc(ge_arg, 1)
            dve.wait_ge(ge_exp, 1)
            link(V.tensor_scalar(hu, hu, 1.0, None, ALU.add))
            link(V.reciprocal(hu, hu))
            V.tensor_tensor(hx, hx, hu, ALU.mult).then_inc(hid_ready, 1)
            u2_evac(5)
            dve.wait_ge(tb_done, tb[0] + 1)
            src = bank(4 + tb[0] % 4)
            link(V.tensor_copy(kcn, src[0:15, 0:192]))
            for i in range(3):
                link(V.tensor_copy(vcr[32 * i:32 * i + 15, :], src[32 * i:32 * i + 15, 256:448]))
            V.tensor_copy(vcr[96:111, :], src[96:111, 256:448]).then_inc(tb_evac, 1)
            tb[0] += 1
            dve.wait_ge(tb_evac, tb[0])
            kt_ = ktmp[0:15, :]
            link(V.tensor_tensor(kt_, kcn, kcn, ALU.mult))
            V.tensor_reduce(ss_h[0:15, 0:3], kt_.rearrange("p (g c) -> p g c", g=3), AX.X, ALU.add).then_inc(kc_ss, 1)
            for b in range(3):
                tb_take(lambda src: V.tensor_copy(kT[:, 512 * b:512 * b + 512], src))
            dve.wait_ge(kc_y0, 1)
            newton(rs_h[0:15, 0:3], ss_h[0:15, 0:3], y0_h[0:15, 0:3], HD)
            k3 = kcn.rearrange("p (g c) -> p g c", g=3)
            link(V.tensor_tensor(k3, k3, bc(rs_h[0:15, 0:3].unsqueeze(2), [15, 3, HD]), ALU.mult))
            link(V.tensor_tensor(k3, k3, bc(gq[0:15, 320:384].unsqueeze(1), [15, 3, HD]), ALU.mult))
            kd = kcd.rearrange("p (g d c) -> p g d c", g=3, d=2)
            t3 = kt_.rearrange("p (g c) -> p g c", g=3)
            cc, sn = cst[0:15, C_KCC:C_KCC + 32], cst[0:15, C_KCS:C_KCS + 32]
            for z in range(2):
                mine, other = k3[:, :, 32 * z:32 * z + 32], k3[:, :, 32 - 32 * z:64 - 32 * z]
                link(V.tensor_tensor(t3[:, :, 0:32], mine, bc(cc.unsqueeze(1), [15, 3, 32]), ALU.mult))
                link(V.tensor_tensor(t3[:, :, 32:64], other, bc(sn.unsqueeze(1), [15, 3, 32]), ALU.mult))
                for d in range(2):
                    link(V.tensor_tensor(kd[:, :, d, 32 * z:32 * z + 32], t3[:, :, 0:32], t3[:, :, 32:64],
                                         ALU.add if z else ALU.subtract))
            signal(kc_ready, 1)
            x = u2[:, :, QB:QB + 768].rearrange("p t (m c) -> p t m c", c=HD)
            head_norm(3, QB, 12, 3, [x])
            u2_evac(6)
            tb_take(lambda src: V.tensor_copy(kcT[:, :], src[:, 0:48]))
            signal(kc_ready, 1)
            head_norm(4, KB, 12, 4, [u2[:, :, KB:KB + 768].rearrange("p t (m c) -> p t m c", c=HD)])
            u2_evac(7)
            dve.wait_ge(sg_exp, 1)
            link(V.tensor_scalar(sgn, sgn, 1.0, None, ALU.add))
            link(V.reciprocal(sgn, sgn))
            s4 = scb[:, :].rearrange("p (t m c) -> p t m c", t=NT, m=12)
            s3 = scb[:, :].rearrange("p (s c) -> p s c", c=CMP_N)
            cma = cst[:, C_CMA:C_CMA + 30].rearrange("p (t c) -> p t c", t=NT)
            cmm = cst[:, C_CMM:C_CMM + 30].rearrange("p (t c) -> p t c", t=NT)
            tb_take(lambda src: V.tensor_tensor(
                s4, src[:, 0:384].rearrange("p (t m c) -> p t m c", t=NT, m=12)[:, :, :, 0:15],
                bc(cma.unsqueeze(2), [P, NT, 12, CMP_N]), ALU.add))
            link(V.tensor_reduce(smax, s3, AX.X, ALU.max))
            V.tensor_tensor(s3, s3, bc(smax.unsqueeze(2), [P, 24, CMP_N]), ALU.subtract).then_inc(cs_arg, 1)
            link(V.memset(pc, 0.0))
            dve.wait_ge(cs_exp, 1)
            link(V.tensor_reduce(cden, s3, AX.X, ALU.add))
            link(V.reciprocal(cden, cden))
            g4 = sgn.rearrange("p (t m b) -> p t m b", t=NT, b=3)
            c3 = cden.rearrange("p (t m) -> p t m", t=NT)
            link(V.tensor_tensor(c3, c3, g4[:, :, :, 0], ALU.mult))
            link(V.tensor_tensor(s4, s4, bc(cmm.unsqueeze(2), [P, NT, 12, CMP_N]), ALU.mult))
            V.tensor_tensor(pc.rearrange("p (s c) -> p s c", c=32)[:, :, 0:15], s3,
                            bc(cden.unsqueeze(2), [P, 24, CMP_N]), ALU.mult).then_inc(pc_ready, 1)
            u2_evac(8)
            tb_take(lambda src: V.tensor_copy(pcT[:, 0:512], src))
            tb_take(lambda src: V.tensor_copy(pcT[:, 512:768], src[:, 0:256]))
            signal(pc_ready, 1)
            for b in range(3):
                t, c = divmod(512 * b, 768)
                if c + 512 <= 768:
                    tb_take(lambda src: V.tensor_copy(xn[:, t, c:c + 512], src))
                else:
                    dve.wait_ge(tb_done, tb[0] + 1)
                    src = bank(4 + tb[0] % 4)
                    link(V.tensor_copy(xn[:, t, c:768], src[:, 0:768 - c]))
                    V.tensor_copy(xn[:, t + 1, 0:c + 512 - 768], src[:, 768 - c:512]).then_inc(tb_evac, 1)
                    tb[0] += 1
                    dve.wait_ge(tb_evac, tb[0])
            for b in range(3):
                tb_take(lambda src: V.tensor_scalar(qbT[:, 512 * b:512 * b + 512], src, 0.125, None, ALU.mult))
            for b in range(3):
                tb_take(lambda src: V.tensor_copy(kbT[:, 512 * b:512 * b + 512], src))

            def post_nsa(n, u):
                k = len(u["segs"])
                nh = k // 2
                t, h0 = u["t"], u["hs"][0]
                link(V.reciprocal(coef[:, 0:k], den_of(n)[0]))
                cv = coef[:, 0:k].rearrange("p (m b) -> p m b", b=2)
                link(V.tensor_tensor(cv, cv, g4[:, t, h0:h0 + nh, 1:3], ALU.mult))
                w = comb2[:, 0:64 * k]
                V.tensor_tensor(w.rearrange("p (s c) -> p s c", c=64),
                                bank(7)[:, 0:64 * k].rearrange("p (s c) -> p s c", c=64),
                                bc(coef[:, 0:k].unsqueeze(2), [P, k, 64]), ALU.mult).then_inc(post_done, 1)
                dve.wait_ge(post_done, n + 1)
                wv = w.rearrange("p (m b c) -> p m b c", b=2, c=64)
                y = xn[:, t, 64 * h0:64 * h0 + 64 * nh].rearrange("p (m c) -> p m c", c=64)
                link(V.tensor_tensor(y, y, wv[:, :, 0], ALU.add))
                link(V.tensor_tensor(y, y, wv[:, :, 1], ALU.add))

            def post_dil(n, u):
                k = len(u["segs"])
                c = 512 + 64 * u["hs"][0]
                V.tensor_copy(u2[:, u["t"], c:c + 64 * k], bank(7)[:, 0:64 * k]).then_inc(post_done, 1)

            gate_cols = [QB, QB + 512, QB + 1024, QA]

            def gate_evac(g):
                s = IN2 + 9 + g
                dve.wait_ge(strip_done, s + 1)
                src = bank(strips[s]["pair"], 2).rearrange("p (t c) -> p t c", t=NT)
                V.tensor_tensor(u2[:, :, gate_cols[g]:gate_cols[g] + 512], src,
                                bc(r45.unsqueeze(2), [P, NT, 512]), ALU.mult).then_inc(evac_done, 1)
                dve.wait_ge(evac_done, strips[s]["evac"])
                signal(gates_in, 1)

            lse = dl[1].rearrange("p (t g i) -> p t g i", t=NT, g=3)
            d8v = [x.rearrange("p (t i) -> p t i", t=NT) for x in d8]

            def dilation_lse():
                dve.wait_ge(post_done, U_N)
                signal(dl_den, 1)
                link(V.reciprocal(dl[2], dil_den))

            def dilation_max():
                dve.wait_ge(dl_ln, 1)
                link(V.tensor_tensor(dl[1], dl[0], dil_nm, ALU.subtract))
                link(V.tensor_reduce(d8v[0], lse.rearrange("p t g i -> p t i g"), AX.X, ALU.max))
                V.tensor_tensor(lse, lse, bc(d8v[0].unsqueeze(2), [P, NT, 3, 4]), ALU.subtract).then_inc(dl_arg, 1)

            def dilation_weights():
                dve.wait_ge(dl_exp, 1)
                link(V.tensor_reduce(d8v[1], lse.rearrange("p t g i -> p t i g"), AX.X, ALU.add))
                link(V.reciprocal(d8[2], d8[1]))
                link(V.tensor_tensor(dl[1], dl[1], dl[2], ALU.mult))
                link(V.tensor_tensor(lse, lse, bc(d8v[2].unsqueeze(2), [P, NT, 3, 4]), ALU.mult))
            def hook2(i):
                if i - U_A in (14, 28):
                    gate_evac(1 + (i - U_A) // 14)
                if i == U_N + 2:
                    dilation_lse()
                if i == U_N + 3:
                    dilation_max()
                if i == U_N + 6:
                    dilation_weights()
                    signal(dl_weights, 1)
                if i == NU:
                    dve.wait_ge(dl_mixed, 2)
                    signal(xn_ready, 3)

            gate_evac(0)
            gate_evac(1)
            unit_loop(U_A, NU, lambda n, u: (post_nsa if u["kind"] == "nsa" else post_dil)(n, u), hook2)
            signal(xn_ready, 1)
            fill_lo()
            dve.wait_ge(gates_sig, 2)
            for b in range(4):
                t, n = b // 2, b % 2
                bank_wait(3, b)
                c = slice(512 * n, 512 * n + 512)
                link(V.tensor_tensor(xn[:, t, c], bank(b), u2[:, t, gate_cols[n]:gate_cols[n] + 512], ALU.mult))
                gb = u2[:, t, gate_cols[2 + n]:gate_cols[2 + n] + 512]
                link(V.tensor_tensor(gb, bank(yb_bank(b)), gb, ALU.mult))
                V.tensor_tensor(xn[:, t, c], xn[:, t, c], gb, ALU.add).then_inc(xn_ready, 1)
            signal(evac_done, 1)
            fill_lo()
            residual(IN2 + 16, gbuf[0])
            fill_lo()
            row_scale(6)
            broadcast_rstd(6, bank(0))
            mlp(MLP2, 8, 1)
            residual(NS - 1, None)

        @block.tensor
        def _(pe):
            T = nc.tensor
            tb = [0]
            ups = [0]
            fills = [0]
            a_n = [0]
            row_n = [0]
            bcasts = [0]

            def switch_rows(last):
                row_n[0] += 1
                last.then_inc(row_step, 1)
                pe.wait_ge(row_step, row_n[0])

            def three(dst, xh, xl, wh, wl, start, stop, w_stationary):
                pairs = [(xh, wh), (xh, wl), (xl, wh)] if not w_stationary else [(xh, wh), (xl, wh), (xh, wl)]
                for i, (x, w) in enumerate(pairs):
                    l, r = (w, x) if w_stationary else (x, w)
                    last = T.matmul(dst, l, r, start=start and i == 0, stop=stop and i == 2)
                return last

            def steps_of(s):
                m = strips[s]["mode"]
                outer = NT if m == "tok" else 4
                inner = 4 if m in ("acc", "down", "mixed") else KT
                return [(o, k) for o in range(outer) for k in range(inner)]

            def strip(s, first=0, last=None, fill_waits={}, i=None):
                def at(count, per_turn):
                    return count if i is None else i * per_turn + count

                steps = steps_of(s)
                last = len(steps) if last is None else last
                d = strips[s]
                m, w = d["mode"], d["w"]
                hi_, lo_ = HI[s % 2], LO[s % 2]
                xh, xl = XH[d["x"]], XL[d["x"]]
                if first == 0:
                    pe.wait_ge(lo_done, at(los(half_of[s][0]), 8))
                    if m == "up":
                        if d["j"] >= 2 or ups[0] >= 8:
                            pe.wait_ge(up_evac, at(ups[0] - 1, 2))
                        ups[0] += 1
                    elif d["need_evac"]:
                        pe.wait_ge(evac_done, d["need_evac"])
                    if m == "down":
                        a_n[0] += 1
                        pe.wait_ge(a_lo, at(a_n[0], 2))
                b0 = 4 + 2 * (d["j"] % 2) if m == "up" else d.get("pair", 0)
                for n_step, (o, k) in enumerate(steps[first:last]):
                    if n_step in fill_waits:
                        pe.wait_ge(tb_evac, fill_waits[n_step])
                    if s == 0 and first + n_step == 0:
                        pe.wait_ge(lo_first, 1)
                    if first + n_step == (2 if m in ("acc", "down", "mixed") else 4):
                        pe.wait_ge(lo_done, at(los(half_of[s][1]), 8))
                        if s == 0:
                            pe.wait_ge(lo_first, 2)
                    if m == "tok":
                        c = 2048 * (k // 4) + w * (k % 4)
                        x0 = S * k + P * o
                        x = three(bank(b0 + o)[:, 0:w], xh[:, x0:x0 + P], xl[:, x0:x0 + P],
                                  hi_[:, c:c + w], lo_[:, c:c + w], k == 0, k == KT - 1, False)
                    elif m in ("T", "up"):
                        c = 2048 * (k // 4) + w * (k % 4) + P * o
                        dst = PS[:, 512 * b0 + S * o:512 * b0 + S * o + S]
                        x = three(dst, xh[:, S * k:S * k + S], xl[:, S * k:S * k + S],
                                  hi_[:, c:c + P], lo_[:, c:c + P], k == 0, k == KT - 1, True)
                    else:
                        t, n = o // 2, o % 2
                        c = 1024 * k + 512 * n
                        x0 = S * (d["k0"] + k) + P * t
                        b = o
                        start, stop = d["first"] and k == 0, d["last"] and k == 3
                        if m == "mixed":
                            start, stop = k == 2, k in (1, 3)
                            b = yb_bank(o) if k >= 2 else o
                        x = three(bank(b), xh[:, x0:x0 + P], xl[:, x0:x0 + P],
                                  hi_[:, c:c + 512], lo_[:, c:c + 512], start, stop, False)
                        if d["last"] and k == 3 and o < 3:
                            x.then_inc(bank_done, 1)
                if last == len(steps):
                    x.then_inc(strip_done, 1)

            def tb_bank():
                n = tb[0]
                if n >= 4:
                    pe.wait_ge(tb_evac, n - 3)
                tb[0] += 1
                return bank(4 + n % 4)

            def fill(k, posts={}):
                for b in range(4):
                    if b in posts:
                        pe.wait_ge(post_done, posts[b])
                    t, kh = b // 2, b % 2
                    pe.wait_ge(xn_ready, 4 * fills[0] + b + 1)
                    dst = tb_bank()
                    for q in range(4):
                        c = P * (4 * kh + q)
                        last = T.transpose(dst[:, P * q:P * q + P], xn[:, t, c:c + P], ident)
                    last.then_inc(tb_done, 1)
                fills[0] += 1

            def broadcast_rstd(dst):
                bcasts[0] += 1
                pe.wait_ge(diag_ready, 2 * bcasts[0])
                T.matmul(dst[:, 0:S], negones, diag, start=True, stop=True).then_inc(rb_done, 1)

            def head_T(src, n_pairs):
                for b in range(n_pairs // 2):
                    dst = tb_bank()
                    for q in range(4):
                        pair, t = 2 * b + q // 2, q % 2
                        last = T.transpose(dst[:, P * q:P * q + P], src(pair, t), ident)
                    last.then_inc(tb_done, 1)

            def unit_loop(n0, n1, hook):
                for i in range(n0, n1 + 2):
                    if i < n1:
                        u = units[i]
                        if i >= 2:
                            pe.wait_ge(ex_done, i - 1)
                        rows, hooked = None, False
                        for si, sg in sorted(enumerate(u["segs"]), key=lambda e: e[1]["row"]):
                            if rows is not None and sg["row"] != rows:
                                row_n[0] += 1
                                last.then_inc(row_step, 1)
                                hook(i)
                                hooked = True
                                pe.wait_ge(row_step, row_n[0])
                            rows = sg["row"]
                            dst = bank(4 + i % 2)[:, u["w"] * si:u["w"] * si + u["w"]]
                            nq = len(sg["qk"])
                            for x, (q, k) in enumerate(sg["qk"]):
                                last = T.matmul(dst, q, k, start=x == 0, stop=x == nq - 1 and not sg["mask"])
                            for c, m in sg["mask"]:
                                last = T.matmul(dst[:, c:c + m.shape[1]], identb, m, start=False, stop=True)
                        last.then_inc(sc_done, 1)
                    if i >= n1 or not hooked:
                        hook(i)
                    if n0 <= i - 1 < n1:
                        pe.wait_ge(ex_done, i)
                        if i - 1 >= 1:
                            pe.wait_ge(pt_done, i - 1)
                        for q in range(4):
                            last = T.transpose(bank(6)[:, P * q:P * q + P],
                                               units[i - 1]["pr"][(i - 1) % 2][:, P * q:P * q + P], ident)
                        last.then_inc(tr_done, 1)
                    if i - 2 >= n0:
                        n = i - 2
                        u = units[n]
                        pe.wait_ge(pt_done, n + 1)
                        if n >= 1:
                            pe.wait_ge(post_done, n)
                        pt = u["pr"][2 + n % 2]
                        nk = u["w"] // P
                        for si, sg in enumerate(u["segs"]):
                            for k in range(nk):
                                c = u["w"] * si + P * k
                                last = T.matmul(bank(7)[:, sg["vw"] * si:sg["vw"] * si + sg["vw"]],
                                                pt[:, c:c + P], sg["v"][k], start=k == 0, stop=k == nk - 1)
                        last.then_inc(pv_done, 1)

            def row_strips(s):
                strip(s, fill_waits={0: tb[0] - 3, 8: tb[0] - 1})
                pe.wait_ge(tb_evac, tb[0])
                strip(s + 1)

            def mlp_products(s0, s1):
                strip(s0)
                broadcast_rstd(bank(0))
                strip(s0 + 1)
                pe.wait_ge(rb_taken, bcasts[0])
                strip(s0 + 2)
                with pe.Fori(0, MLP_TURNS) as i:
                    for s in range(s0 + 3, s0 + 7):
                        strip(s, i=i)
                ups[0] += 2 * (MLP_TURNS - 1)
                a_n[0] += 2 * (MLP_TURNS - 1)
                strip(s1 - 1)

            pe.wait_ge(cst_loaded, 16)
            fill(0)
            strip(0, fill_waits={0: tb[0] - 2, 8: tb[0]})
            strip(1)
            strip(2)
            strip(3)
            broadcast_rstd(bank(4))
            pe.wait_ge(rb_taken, 1)
            fill(1)
            pe.wait_ge(qk_ready, 2)
            for u in (u_qa, u_ka):
                head_T(lambda pair, t: u[:, t, P * pair:P * pair + P], 4)
            strip(4)
            strip(5)
            pe.wait_ge(masks_ready, 2)
            pe.wait_ge(tb_evac, tb[0])
            pe.wait_ge(evac_done, strips[2]["evac"])

            def hook1(i):
                strip(6 + i // 4, 8 * (i % 4), 8 * (i % 4) + 8)

            unit_loop(0, U_X, hook1)

            def z_scores(j):
                if j >= 2:
                    pe.wait_ge(z_at, j - 1)
                b = bank(4 + 2 * (j % 2), 2)
                for hh in range(2):
                    if hh:
                        switch_rows(last)
                    r = slice(64 * hh, 64 * hh + 64)
                    for kt in range(2):
                        w = S - P * kt
                        c = 512 * kt + w * hh
                        T.matmul(b[:, c:c + w], ksT[r, S * j + P * kt:S * j + P * kt + P],
                                 qsT[r, S * j + P * kt:S * j + S], start=hh == 0, stop=True, skip_group_check=True)
                        last = T.matmul(b[:, c:c + P], identb, maskb(C_STR, P), start=False, stop=True,
                                        skip_group_check=True)
                last.then_inc(z_done, 1)

            def z_sums(j):
                pe.wait_ge(z_sp, j + 1)
                b, sp = bank(4 + 2 * (j % 2), 2), sbz[j % 2]
                for hh in range(2):
                    T.matmul(b[:, S * hh:S * hh + S], tri, sp[:, S * hh:S * hh + S], start=False, stop=True,
                             skip_group_check=True)
                    T.matmul(b[:, S * hh + P:S * hh + S], negones, sp[:, 512 + P * hh:512 + P * hh + P],
                             start=False, stop=True, skip_group_check=True)
                    last = T.matmul(b[:, 512 + P * hh:512 + P * hh + P], tri, sp[:, 512 + P * hh:512 + P * hh + P],
                                    start=False, stop=True, skip_group_check=True)
                last.then_inc(z_cum, 1)

            def z_out(j):
                pe.wait_ge(z_at, j + 1)
                w = sba[j % 2]
                for hh in range(2):
                    c = 64 * (2 * j + hh)
                    T.matmul(bank(2)[:, c:c + 64], w[:, S * hh:S * hh + P], u_vs[:, 0, c:c + 64], start=True, stop=True)
                    T.matmul(bank(3)[:, c:c + 64], w[:, S * hh + P:S * hh + S], u_vs[:, 0, c:c + 64],
                             start=True, stop=False)
                    last = T.matmul(bank(3)[:, c:c + 64], w[:, 512 + P * hh:512 + P * hh + P],
                                    u_vs[:, 1, c:c + 64], start=False, stop=True)
                last.then_inc(z_pv, 1)

            pe.wait_ge(post_done, U_X)
            for half in range(2):
                z_scores(2 * half)
                z_scores(2 * half + 1)
                strip(8 + half, 0, 12)
                z_sums(2 * half)
                z_sums(2 * half + 1)
                strip(8 + half, 12)
                pe.wait_ge(evac_done, strips[7]["evac"])
                z_out(2 * half)
                z_out(2 * half + 1)
            fill(2)
            row_strips(10)
            fill(3)
            pe.wait_ge(tb_evac, tb[0])
            strip(12)
            broadcast_rstd(bank(7))
            strip(13)
            pe.wait_ge(evac_done, strips[13]["evac"])
            unit_loop(U_X, U_A, lambda i: None)
            fill(4, {3: U_A})
            row_strips(14)
            fill(5)
            pe.wait_ge(tb_evac, tb[0])
            mlp_products(MLP1, IN2)
            pe.wait_ge(up_evac, 8)
            fill(6)
            strip(IN2, fill_waits={0: tb[0] - 2, 8: tb[0]})
            for c in range(1, 4):
                strip(IN2 + c)
            dst = tb_bank()
            pe.wait_ge(misc_loaded, 16 * 16)
            T.transpose(dst[:, 0:32], vecs[0:32, :], ident[0:32, 0:32]).then_inc(tb_done, 1)
            pe.wait_ge(at_ready, 1)
            cd = [cdup[:, 768 * i:768 * i + 768].rearrange("p (t g c) -> p t g c", t=NT, g=3) for i in range(2)]
            head_T(lambda pair, t: cd[pair // 3][:, t, pair % 3, :], 6)
            pe.wait_ge(hn_done, 1)
            head_T(lambda pair, t: u2[:, t, QA + P * pair:QA + P * pair + P], 6)
            strip(IN2 + 4)
            pe.wait_ge(at_ready, 2)
            dst = tb_bank()
            pe.wait_ge(w1_loaded, 16 * len(W1_PARTS))
            raw_wait(pe, RAW_W1)
            w1 = [[RAW[RAW_W1 % 3][:, 256 * k:256 * k + 256] for k in range(8)], []]
            for place, name, _, nk in W1_PARTS:
                w1[name == "cmp_v_w1_2"] += [place[:, k, :] for k in range(nk)]
            for kv in range(2):
                for half in range(2):
                    o = dst[:, 90 * kv + 45 * half:90 * kv + 45 * half + 45]
                    for k in range(16):
                        w = w1[kv][k][:, P * half:P * half + P]
                        last = T.matmul(o, w, AT[:, 720 * kv + 45 * k:720 * kv + 45 * k + 45],
                                        start=k == 0, stop=k == 15)
                if kv == 0:
                    last.then_inc(raw_used, 1)
            last.then_inc(tb_done, 1)
            strip(IN2 + 5)
            pe.wait_ge(hid_ready, 1)
            dst = tb_bank()
            for kv in range(2):
                for g in range(3):
                    for i in range(1 if kv == 0 else 4):
                        o = dst[32 * i:32 * i + 15, 256 * kv + 64 * g:256 * kv + 64 * g + 64]
                        for half in range(2):
                            c = 90 * kv + 45 * half + 15 * g
                            last = T.matmul(o, hx[:, c:c + 15], w2sb[:, kv, half, :], start=half == 0, stop=half == 1)
            last.then_inc(tb_done, 1)
            pe.wait_ge(hn_done, 3)
            kd = [b.rearrange("p (t g c) -> p t g c", t=NT, g=3) for b in kdup]
            head_T(lambda pair, t: kd[pair // 3][:, t, pair % 3, :], 6)
            strip(IN2 + 6)
            pe.wait_ge(kc_ready, 1)
            dst = tb_bank()
            for g in range(3):
                last = T.transpose(dst[:, 16 * g:16 * g + 15], kcd[:, P * g:P * g + P], ident[0:15, 0:15])
            last.then_inc(tb_done, 1)
            strip(IN2 + 7)
            pe.wait_ge(kc_ready, 2)
            dst = tb_bank()
            for odd in range(2):
                if odd:
                    switch_rows(last)
                for hh, t in [(hh, t) for hh in range(odd, 12, 2) for t in range(NT)]:
                    r = slice(64 * (hh % 2), 64 * (hh % 2) + 64)
                    c = 16 * (12 * t + hh)
                    q = qT[r, 256 * (hh // 2) + P * t:256 * (hh // 2) + P * t + P]
                    last = T.matmul(dst[:, c:c + 15], q, kcT[r, 16 * (hh // 4):16 * (hh // 4) + 15],
                                    start=True, stop=True)
            last.then_inc(tb_done, 1)
            strip(IN2 + 8)
            pe.wait_ge(pc_ready, 1)
            for lo4, hi4 in ((0, 4), (4, 6)):
                dst = tb_bank()
                for q in range(lo4, hi4):
                    last = T.transpose(dst[:, P * (q - lo4):P * (q - lo4) + P], pc[:, P * q:P * q + P], ident)
                last.then_inc(tb_done, 1)
            strip(IN2 + 9)
            pe.wait_ge(pc_ready, 2)
            dsts = [tb_bank() for _ in range(3)]
            for row in range(4):
                if row:
                    switch_rows(last)
                for b, dst in enumerate(dsts):
                    for q in (row, row + 4):
                        t, hh = divmod(8 * b + q, 12)
                        r = slice(32 * row, 32 * row + 15)
                        g = hh // 4
                        last = T.matmul(dst[:, 64 * q:64 * q + 64], pcT[r, P * (3 * t + g):P * (3 * t + g) + P],
                                        vcr[r, 64 * g:64 * g + 64], start=True, stop=True)
                    if row == 3:
                        last.then_inc(tb_done, 1)
            pe.wait_ge(hn_done, 4)
            head_T(lambda pair, t: u2[:, t, QB + P * pair:QB + P * pair + P], 6)
            strip(IN2 + 10)
            pe.wait_ge(hn_done, 5)
            head_T(lambda pair, t: u2[:, t, KB + P * pair:KB + P * pair + P], 6)
            pe.wait_ge(tb_evac, tb[0])

            def hook2(i):
                k = (i - U_A) % 14
                if i - U_A < 28:
                    strip(IN2 + 11 + (i - U_A) // 14, 16 * k // 14, 16 * (k + 1) // 14)

            unit_loop(U_A, NU, hook2)
            assert tb[0] == TB_Y2, tb[0]
            fill(7, {2: NU})
            row_strips(IN2 + 13)
            fill(8)
            row_strips(IN2 + 15)
            fill(9)
            pe.wait_ge(tb_evac, tb[0])
            mlp_products(MLP2, NS)


def _pieces():
    rest, out = 2 * math.pi, []
    for bits in (8, 9, 9):
        e = math.floor(math.log2(rest))
        q = 2.0 ** (e - bits + 1)
        p = math.floor(rest / q) * q
        out.append(p)
        rest -= p
    return out + [float(np.float32(rest))]


TWO_PI = _pieces()
PI_LOW = float(np.nextafter(np.float32(math.pi), np.float32(0)))
TB_Y2 = 57

_INS = ["x", "mem", "positions", "g_mix", "w_in", "lambda_q1", "lambda_k1", "lambda_q2", "lambda_k2",
        "g_subln", "w_out", "g_cross", "g_mem", "w_xq", "w_xkv", "w_xo", "g_mlp", "w_up", "w_down",
        "g_final", "norm1_g_2", "w_in_2", "q_norm_a_2", "k_norm_cmp_2", "k_norm_slc_2", "k_norm_win_2",
        "cmp_k_pos_2", "cmp_k_w1_2", "cmp_k_w2_2", "cmp_v_pos_2", "cmp_v_w1_2", "cmp_v_w2_2",
        "q_norm_b_2", "k_norm_b_2", "w_o_a_2", "w_o_b_2", "w_out_2", "norm2_g_2", "w_up_2", "w_down_2"]


def kernel(**inputs):
    import numpy as _np
    import concourse.bacc as _bacc
    from concourse import mybir as _mybir
    from concourse.bass_utils import run_bass_kernel_spmd as _run

    nc = _bacc.Bacc("TRN2", target_bir_lowering=False, num_devices=1, dynamic_dma_scratch_size=1024)
    arrays, aps = {}, {}
    for name in _INS:
        v = _np.ascontiguousarray(inputs[name])
        arrays[f"in_{name}"] = v
        aps[name] = nc.dram_tensor(f"in_{name}", v.shape, _mybir.dt.from_np(v.dtype), kind="ExternalInput").ap()
    arrays["in_cst"] = constants()
    aps["cst"] = nc.dram_tensor("in_cst", arrays["in_cst"].shape, _mybir.dt.float32, kind="ExternalInput").ap()
    out = nc.dram_tensor("out", (1, S, D), _mybir.dt.float32, kind="ExternalOutput").ap()
    build(nc, aps, out)
    r = _run(nc, [arrays], core_ids=[0])
    return r.results[0]["out"]
```
